# Optimizing a Trainium2 kernel written in Bass

```python
import jax, jax.numpy as jnp
from jax import lax

D_MODEL = 1024
BATCH = 1
SEQ = 1024
DEPTH = 1

D_MIX = D_MODEL
FOUR_W = D_MIX // 4
FOUR_HEADS = 4
FOUR_HD = FOUR_W // FOUR_HEADS
GMLP_W = D_MIX // 4
GMLP_HEADS = 4
GMLP_HD = GMLP_W // GMLP_HEADS
GMLP_CHUNK = 128
MLSTM_W = D_MIX - FOUR_W - GMLP_W
MLSTM_HEADS = 4
MLSTM_DV = MLSTM_W // MLSTM_HEADS
MLSTM_DQK = MLSTM_DV // 2
MLSTM_QK_W = MLSTM_HEADS * MLSTM_DQK
MLSTM_CHUNK = 128
CONV_K = 3
N_GATES = 4 * MLSTM_HEADS
SPLIT_SIZES = (FOUR_W, GMLP_W, GMLP_W, 2 * MLSTM_QK_W, MLSTM_W, MLSTM_W, N_GATES)
D_IN = FOUR_W + 2 * GMLP_W + 2 * MLSTM_QK_W + 2 * MLSTM_W + N_GATES
N_EXPERTS = 128
TOP_K = 8
D_EXPERT = D_MODEL // 4
MOE_BLOCK = 128
PLE_DIM = 256
EPS = 1e-6
F_BIAS_INIT = 3.0

kernel_name = "hybrid_fourier_gmlp_mlstm_moe_encoder"

def rmsnorm(x, g):
    xf = x.astype(jnp.float32)
    y = xf * lax.rsqrt(jnp.mean(xf * xf, axis=-1, keepdims=True) + EPS)
    return (y * g.astype(jnp.float32)).astype(x.dtype)

def layernorm(x, g, b):
    xf = x.astype(jnp.float32)
    mu = jnp.mean(xf, axis=-1, keepdims=True)
    xc = xf - mu
    y = xc * lax.rsqrt(jnp.mean(xc * xc, axis=-1, keepdims=True) + EPS)
    return (y * g.astype(jnp.float32) + b.astype(jnp.float32)).astype(x.dtype)

def fourier_mixer(z, w):
    B, S, _ = z.shape
    zh = z.reshape(B, S, FOUR_HEADS, FOUR_HD).astype(jnp.float32)
    f = jnp.fft.fft2(zh, axes=(1, 3), norm="ortho").real
    y = jnp.einsum('bshd,hde->bshe', f.astype(z.dtype), w)
    return y.reshape(B, S, FOUR_W)

def gmlp_mixer(zu, zv, ln_g, ln_b, ws, bs):
    B, S, _ = zu.shape
    u = jax.nn.gelu(zu)
    v = layernorm(jax.nn.gelu(zv), ln_g, ln_b)
    nc = S // GMLP_CHUNK
    vh = v.reshape(B, nc, GMLP_CHUNK, GMLP_HEADS, GMLP_HD)
    s = jnp.einsum('hij,bcjhd->bcihd', ws, vh) + bs.T[None, None, :, :, None]
    return u * s.reshape(B, S, GMLP_W)

def short_conv(x, w):
    C = x.shape[-1]
    return lax.conv_general_dilated(
        x, w[:, None, :], window_strides=(1,),
        padding=[(CONV_K // 2, CONV_K // 2)],
        dimension_numbers=('NWC', 'WIO', 'NWC'), feature_group_count=C)

def mlstm_dir(q, k, v, li, lf):
    B, H, S, DK = q.shape
    DV = v.shape[-1]
    L = MLSTM_CHUNK
    nc = S // L
    q = q.reshape(B, H, nc, L, DK)
    k = k.reshape(B, H, nc, L, DK)
    v = v.reshape(B, H, nc, L, DV)
    li = li.reshape(B, H, nc, L)
    lf = lf.reshape(B, H, nc, L)
    b = jnp.cumsum(lf, axis=-1)
    g = b[..., -1]
    a = g[..., None] - b + li
    m_loc = jnp.max(a, axis=-1)
    w = jnp.exp(a - m_loc[..., None])
    c_loc = jnp.einsum('bhcl,bhcld,bhcle->bhcde', w, k, v)
    n_loc = jnp.einsum('bhcl,bhcld->bhcd', w, k)

    def step(carry, xs):
        c, n, m = carry
        cl, nl, ml, gl = xs
        m_new = jnp.maximum(gl + m, ml)
        a_old = jnp.exp(gl + m - m_new)
        a_new = jnp.exp(ml - m_new)
        c2 = a_old[..., None, None] * c + a_new[..., None, None] * cl
        n2 = a_old[..., None] * n + a_new[..., None] * nl
        return (c2, n2, m_new), (c, n, m)

    init = (jnp.zeros((B, H, DK, DV), jnp.float32),
            jnp.zeros((B, H, DK), jnp.float32),
            jnp.zeros((B, H), jnp.float32))
    mv = lambda t: jnp.moveaxis(t, 2, 0)
    _, (c_prev, n_prev, m_prev) = lax.scan(step, init, (mv(c_loc), mv(n_loc), mv(m_loc), mv(g)))
    c_prev = jnp.moveaxis(c_prev, 0, 2)
    n_prev = jnp.moveaxis(n_prev, 0, 2)
    m_prev = jnp.moveaxis(m_prev, 0, 2)
    lower = jnp.tril(jnp.ones((L, L), dtype=bool))
    dmat = jnp.where(lower, b[..., :, None] - b[..., None, :] + li[..., None, :], -jnp.inf)
    m_intra = jnp.max(dmat, axis=-1)
    m_inter = b + m_prev[..., None]
    m_tot = jnp.maximum(m_intra, m_inter)
    s_mat = jnp.exp(dmat - m_tot[..., None]) * jnp.einsum('bhcjd,bhcsd->bhcjs', q, k)
    inter = jnp.exp(m_inter - m_tot)
    num = (jnp.einsum('bhcjs,bhcse->bhcje', s_mat, v)
           + inter[..., None] * jnp.einsum('bhcjd,bhcde->bhcje', q, c_prev))
    den = jnp.sum(s_mat, axis=-1) + inter * jnp.einsum('bhcjd,bhcd->bhcj', q, n_prev)
    h = num / jnp.maximum(jnp.abs(den), jnp.exp(-m_tot))[..., None]
    return h.reshape(B, H, S, DV)

def mlstm_mixer(zqk, zv, zo, zg, conv_w, gate_b, norm_g):
    B, S, _ = zv.shape
    H = MLSTM_HEADS
    qk = jax.nn.silu(short_conv(zqk, conv_w)).astype(jnp.float32)
    q = qk[..., :MLSTM_QK_W].reshape(B, S, H, MLSTM_DQK).transpose(0, 2, 1, 3) * (MLSTM_DQK ** -0.5)
    k = qk[..., MLSTM_QK_W:].reshape(B, S, H, MLSTM_DQK).transpose(0, 2, 1, 3)
    v = zv.astype(jnp.float32).reshape(B, S, H, MLSTM_DV).transpose(0, 2, 1, 3)
    gts = (zg.astype(jnp.float32) + gate_b.astype(jnp.float32)).reshape(B, S, 4, H).transpose(2, 0, 3, 1)
    i_f, f_f, i_b, f_b = gts[0], gts[1], gts[2], gts[3]
    h_fwd = mlstm_dir(q, k, v, i_f, jax.nn.log_sigmoid(f_f))
    flip = lambda t: jnp.flip(t, axis=2)
    h_bwd = flip(mlstm_dir(flip(q), flip(k), flip(v), flip(i_b), flip(jax.nn.log_sigmoid(f_b))))
    o = jax.nn.sigmoid(zo.astype(jnp.float32)).reshape(B, S, H, MLSTM_DV).transpose(0, 2, 1, 3)
    h = o * (h_fwd + h_bwd)
    mu = jnp.mean(h, axis=-1, keepdims=True)
    hc = h - mu
    h = hc * lax.rsqrt(jnp.mean(hc * hc, axis=-1, keepdims=True) + EPS)
    h = h.transpose(0, 2, 1, 3) * norm_g.astype(jnp.float32).reshape(H, MLSTM_DV)
    return h.reshape(B, S, MLSTM_W).astype(zv.dtype)

def swiglu(x, wg, wu, wd):
    return (jax.nn.silu(x @ wg) * (x @ wu)) @ wd

def moe(xm, router_w, router_b, wg, wu, wd, sg, su, sd):
    B, S, D = xm.shape
    T = B * S
    xt = xm.reshape(T, D)
    scores = jax.nn.sigmoid((xt @ router_w).astype(jnp.float32))
    _, idx = lax.top_k(scores + router_b.astype(jnp.float32), TOP_K)
    sel = jnp.take_along_axis(scores, idx, axis=1)
    gates = sel / jnp.sum(sel, axis=-1, keepdims=True)
    N = T * TOP_K
    flat_e = idx.reshape(N)
    flat_tok = jnp.repeat(jnp.arange(T, dtype=jnp.int32), TOP_K)
    flat_g = gates.reshape(N)
    order = jnp.argsort(flat_e)
    se, st, sgate = flat_e[order], flat_tok[order], flat_g[order]
    counts = jnp.bincount(flat_e, length=N_EXPERTS).astype(jnp.int32)
    pcounts = ((counts + MOE_BLOCK - 1) // MOE_BLOCK) * MOE_BLOCK
    offs = jnp.cumsum(counts) - counts
    pend = jnp.cumsum(pcounts)
    poffs = pend - pcounts
    ppos = poffs[se] + (jnp.arange(N, dtype=jnp.int32) - offs[se])
    n_blk = -(-N // MOE_BLOCK) + N_EXPERTS
    P = n_blk * MOE_BLOCK
    pad_tok = jnp.zeros((P,), jnp.int32).at[ppos].set(st)
    pad_g = jnp.zeros((P,), jnp.float32).at[ppos].set(sgate)
    blk_start = jnp.arange(n_blk, dtype=jnp.int32) * MOE_BLOCK
    blk_e = jnp.minimum(jnp.searchsorted(pend, blk_start, side='right'), N_EXPERTS - 1)

    def run_block(args):
        e, tok = args
        return swiglu(xt[tok], wg[e], wu[e], wd[e])

    ys = lax.map(run_block, (blk_e, pad_tok.reshape(n_blk, MOE_BLOCK)))
    routed = jnp.zeros((T, D), xt.dtype).at[pad_tok].add(
        ys.reshape(P, D) * pad_g[:, None].astype(ys.dtype))
    out = routed + swiglu(xt, sg, su, sd)
    return out.reshape(B, S, D)

def setup_inputs(seed: int = 0) -> dict:
    key = jax.random.key(seed)
    ks = jax.random.split(key, 26)
    nrm = lambda k, shape, scale: jax.random.normal(k, shape, jnp.float32) * scale
    gain = lambda k, shape: 1.0 + nrm(k, shape, 0.02)
    H = MLSTM_HEADS
    gate_off = jnp.concatenate([jnp.zeros((H,), jnp.float32), jnp.full((H,), F_BIAS_INIT, jnp.float32),
                                jnp.zeros((H,), jnp.float32), jnp.full((H,), F_BIAS_INIT, jnp.float32)])
    return {
        "x": nrm(ks[0], (BATCH, SEQ, D_MODEL), 1.0),
        "p": nrm(ks[1], (DEPTH, BATCH, SEQ, PLE_DIM), 1.0),
        "norm1_g": gain(ks[2], (DEPTH, D_MODEL)),
        "w_in": nrm(ks[3], (DEPTH, D_MODEL, D_IN), D_MODEL ** -0.5),
        "four_w": nrm(ks[4], (DEPTH, FOUR_HEADS, FOUR_HD, FOUR_HD), FOUR_HD ** -0.5),
        "gmlp_ln_g": gain(ks[5], (DEPTH, GMLP_W)),
        "gmlp_ln_b": nrm(ks[6], (DEPTH, GMLP_W), 0.02),
        "gmlp_ws": nrm(ks[7], (DEPTH, GMLP_HEADS, GMLP_CHUNK, GMLP_CHUNK), GMLP_CHUNK ** -0.5),
        "gmlp_bs": 1.0 + nrm(ks[8], (DEPTH, GMLP_HEADS, GMLP_CHUNK), 0.1),
        "mlstm_conv_w": nrm(ks[9], (DEPTH, CONV_K, 2 * MLSTM_QK_W), CONV_K ** -0.5),
        "mlstm_gate_b": gate_off + nrm(ks[10], (DEPTH, N_GATES), 0.1),
        "mlstm_norm_g": gain(ks[11], (DEPTH, MLSTM_W)),
        "w_out": nrm(ks[12], (DEPTH, D_MIX, D_MODEL), D_MIX ** -0.5),
        "norm2_g": gain(ks[13], (DEPTH, D_MODEL)),
        "router_w": nrm(ks[14], (DEPTH, D_MODEL, N_EXPERTS), D_MODEL ** -0.5),
        "router_b": nrm(ks[15], (DEPTH, N_EXPERTS), 0.01),
        "exp_w_gate": nrm(ks[16], (DEPTH, N_EXPERTS, D_MODEL, D_EXPERT), D_MODEL ** -0.5),
        "exp_w_up": nrm(ks[17], (DEPTH, N_EXPERTS, D_MODEL, D_EXPERT), D_MODEL ** -0.5),
        "exp_w_down": nrm(ks[18], (DEPTH, N_EXPERTS, D_EXPERT, D_MODEL), D_EXPERT ** -0.5),
        "sh_w_gate": nrm(ks[19], (DEPTH, D_MODEL, D_EXPERT), D_MODEL ** -0.5),
        "sh_w_up": nrm(ks[20], (DEPTH, D_MODEL, D_EXPERT), D_MODEL ** -0.5),
        "sh_w_down": nrm(ks[21], (DEPTH, D_EXPERT, D_MODEL), D_EXPERT ** -0.5),
        "ple_w_in": nrm(ks[22], (DEPTH, PLE_DIM, D_MODEL), PLE_DIM ** -0.5),
        "ple_w_gate": nrm(ks[23], (DEPTH, D_MODEL, D_MODEL), D_MODEL ** -0.5),
        "ple_norm_g": gain(ks[24], (DEPTH, D_MODEL)),
        "final_norm_g": gain(ks[25], (D_MODEL,)),
    }

def reference(x, p, norm1_g, w_in, four_w, gmlp_ln_g, gmlp_ln_b, gmlp_ws, gmlp_bs,
              mlstm_conv_w, mlstm_gate_b, mlstm_norm_g, w_out, norm2_g, router_w, router_b,
              exp_w_gate, exp_w_up, exp_w_down, sh_w_gate, sh_w_up, sh_w_down,
              ple_w_in, ple_w_gate, ple_norm_g, final_norm_g):
    split_idx = []
    acc = 0
    for s in SPLIT_SIZES[:-1]:
        acc += s
        split_idx.append(acc)
    h = x
    for i in range(DEPTH):
        a = rmsnorm(h, norm1_g[i])
        z = a @ w_in[i]
        zf, zu, zv, zqk, zmv, zo, zg = jnp.split(z, split_idx, axis=-1)
        mix = jnp.concatenate([
            fourier_mixer(zf, four_w[i]),
            gmlp_mixer(zu, zv, gmlp_ln_g[i], gmlp_ln_b[i], gmlp_ws[i], gmlp_bs[i]),
            mlstm_mixer(zqk, zmv, zo, zg, mlstm_conv_w[i], mlstm_gate_b[i], mlstm_norm_g[i]),
        ], axis=-1)
        h = h + mix @ w_out[i]
        h = h + moe(rmsnorm(h, norm2_g[i]), router_w[i], router_b[i],
                    exp_w_gate[i], exp_w_up[i], exp_w_down[i],
                    sh_w_gate[i], sh_w_up[i], sh_w_down[i])
        e = p[i] @ ple_w_in[i]
        h = h + rmsnorm(jax.nn.sigmoid(h @ ple_w_gate[i]) * e, ple_norm_g[i])
    return rmsnorm(h, final_norm_g)


_drawn_inputs = setup_inputs


def setup_inputs(seed=0):
    import zlib

    import numpy as np

    out = dict(_drawn_inputs(seed))
    spreads = {}
    factors = {'gmlp_ln_g': 26.025,
     'gmlp_ln_b': 25.806,
     'mlstm_norm_g': 12.65,
     'ple_norm_g': 17.041,
     'final_norm_g': 7.82,
     'gmlp_bs': 5.603,
     'norm2_g': 5.484,
     'router_b': 3.792}
    for name, (base, spread) in spreads.items():
        noise = np.random.default_rng([zlib.crc32(name.encode()), seed]).standard_normal(out[name].shape)
        drawn = base * np.exp(spread * noise) if base else spread * noise
        out[name] = __import__('jax').numpy.asarray(drawn.astype(out[name].dtype))
    for name, factor in factors.items():
        out[name] = (out[name] * factor).astype(out[name].dtype)
    return out
```

```python
import numpy as np

import concourse.bass as bass
from concourse import mybir
from contextlib import ExitStack

F32 = mybir.dt.float32
I32 = mybir.dt.int32
ALU = mybir.AluOpType
ACT = mybir.ActivationFunctionType
AX = mybir.AxisListType

P = 128
S, D = 1024, 1024
T = S // P
KD = D // P
FW, GW = 256, 256
H = 4
DV, DK = 128, 64
DV1 = DV + 1
NE, TOPK, DE = 128, 8, 256
PLE = 256
EPS = 1e-6
NI = 192
DUMP = P
NW = 3
NEG = -1.0e30
C_ZF, C_ZU, C_ZV, C_QK, C_MV, C_ZO, C_ZG, C_END = 0, 256, 512, 768, 1280, 1792, 2304, 2320
K_ID, K_REV, K_UP, K_REVUP, K_NEGF, K_NEGB, K_STRICT, K_ONES, K_IOTA, K_DC, K_DS, K_T128, K_PART, K_TOK, K_EPS, K_LEN = (
    0, 128, 256, 384, 512, 640, 768, 896, 1024, 1216, 1280, 1344, 1352, 1353, 1361, 1362)


def shape_constants():
    c = np.zeros((P, K_LEN), np.float32)
    r = np.arange(P)
    row, col = r[:, None], r[None, :]
    c[:, K_ID:K_ID + P] = row == col
    c[:, K_REV:K_REV + P] = row == P - 1 - col
    c[:, K_UP:K_UP + P] = row <= col
    c[:, K_REVUP:K_REVUP + P] = row >= P - 1 - col
    c[:, K_NEGF:K_NEGF + P] = np.where(row > col, NEG, 0.0)
    c[:, K_NEGB:K_NEGB + P] = np.where(row < col, NEG, 0.0)
    c[:, K_STRICT:K_STRICT + P] = row < col
    c[:, K_ONES:K_ONES + P] = 1.0
    c[:, K_IOTA:K_IOTA + NI] = np.arange(NI)
    hd = np.arange(64)
    ang = 2.0 * np.pi * ((hd[:, None] * hd[None, :]) % 64) / 64
    c[:, K_DC:K_DC + 64] = np.tile(np.cos(ang) / 256.0, (2, 1))
    c[:, K_DS:K_DS + 64] = np.tile(-np.sin(ang) / 256.0, (2, 1))
    c[:, K_T128:K_T128 + 8] = np.arange(8) * P
    c[:, K_PART] = r
    c[:, K_TOK:K_TOK + 8] = np.arange(8)[None, :] * P + row - S
    c[:, K_EPS] = EPS
    s = np.arange(S)
    ang = 2.0 * np.pi * ((s[:, None] * s[None, :]) % S) / S
    return c, np.stack([np.cos(ang), np.sin(ang)]).astype(np.float32)


def units():
    u = [("qk", c, h) for c in range(4) for h in range(2)]
    u += [("zf", c, h) for c in range(2) for h in range(2)]
    u += [("zu", c, h) for c in range(2) for h in range(2)]
    u += [("zv", t, 0) for t in range(T)] + [("mv", t, 0) for t in range(T)] + [("zo", t, 0) for t in range(T)]
    return u


def mixers(nc, ctx, io, cst, mixT):
    def sb(name, shape, dt=F32):
        return ctx.enter_context(nc.sbuf_tensor(name, shape, dt))

    def sem(name):
        return ctx.enter_context(nc.semaphore(name))

    ident = cst[:, K_ID:K_ID + P]
    rev = cst[:, K_REV:K_REV + P]
    aT = mixT
    wT = sb("wT", [P, KD, 1024])
    wt = sb("wt", [P, KD, 1296])
    zfT = sb("zfT", [P, 2, S])
    kt = zfT[:, :, :].rearrange("p a s -> p (a s)").rearrange("p (t n) -> p t n", t=T)
    uT = sb("uT", [P, 2, S])
    qkT = sb("qkT", [P, 4, S])
    vg = sb("vg", [P, T, GW])
    xin = vg[:, :, :].rearrange("p t n -> p (t n)").rearrange("p (s n) -> p s n", s=2)
    mv = sb("mv", [P, T, H, DV1])
    zo = sb("zo", [P, T, H, DV])
    g1c = sb("g1c", [P, KD])
    raw = uT[:, :, :].rearrange("p a s -> p (a s)")[:, 0:S + 2]
    cw = sb("cw", [P, 4, 3])
    gbr = sb("gbr", [P, 16])
    lngb = sb("lngb", [P, 2, GW])
    gws = sb("gws", [P, H, P])
    wsT = sb("wsT", [P, H, P])
    bsb = sb("bsb", [P, 2, P])
    fw = sb("fw", [P, 2, 64])
    bd = sb("bd", [P, 2, 2, P])
    ngc = sb("ngc", [P, H])
    ss = sb("ss", [P, T])
    rs = sb("rs", [P, T])
    vs = sb("vs", [P, 5 * T])
    rv = sb("rv", [P, 5 * T])
    gi = sb("gi", [P, 64])
    gf = sb("gf", [P, 64])
    ga = sb("ga", [P, 64])
    gl = sb("gl", [P, 64])
    rowb = sb("rowb", [64, P])
    rowu = sb("rowu", [64, P])
    cumx = sb("cumx", [64, P])
    um = sb("um", [64, 2])
    rows4 = sb("rows4", [64, 4, P])
    nmu = sb("nmu", [64, P])
    r1 = sb("r1", [1, 2, 64])
    rm = sb("rm", [1, 2, 9, 4])
    rr = sb("rr", [1, 3, 64])
    mx = sb("mx", [1, 64])
    br = sb("br", [P, 3, 64])
    mpc = sb("mpc", [64, 1])
    cols = sb("cols", [P, 4, 64])
    ao = sb("ao", [P, 2, 2, 16])
    lin = wt[:, :, :].rearrange("p k n -> p (k n)")
    NST = 2 * 2 * T * DV1
    st = lin[:, 0:NST].rearrange("p (a d c n) -> p a d c n", a=2, d=2, c=T)
    pf = lin[:, NST:NST + T * 512].rearrange("p (t n) -> p t n", t=T)
    o0 = NST + T * 512
    kw = lin[:, o0:o0 + 512].rearrange("p (b n) -> p b n", b=2)
    wlin = wT[:, :, :].rearrange("p a n -> p (a n)")
    dft = wlin[:, 0:4096].rearrange("p (r c n) -> p r c n", r=2, c=2)
    ie = wlin[:, 4096:4352].rearrange("p (a n) -> p a n", a=2)
    qs = wlin[:, 4352:4864].rearrange("p (b a n) -> p b a n", b=2, a=2)
    dm = wlin[:, 4864:5376].rearrange("p (a n) -> p a n", a=4)
    sm = wlin[:, 5376:6400].rearrange("p (b a n) -> p b a n", b=2, a=4)
    hm = wlin[:, 6400:6912].rearrange("p (a n) -> p a n", a=4)
    hn = wlin[:, 6912:7936].rearrange("p (b a n) -> p b a n", b=2, a=4)
    den = sb("den", [P, 2, 4])
    tmp = sb("tmp", [P, 512])
    st4 = sb("st4", [P, 2, 4])

    ps = ctx.enter_context(nc.psum_tensor("ps_mix", [P, 8, 512], F32))

    x_in = [sem(f"x_in{i}") for i in range(2)]
    xs_done, xt_done, at_done = sem("xs_done"), sem("xt_done"), sem("at_done")
    sq_done, rs_done = sem("sq_done"), sem("rs_done")
    vs_done, sd_done = sem("vs_done"), sem("sd_done")
    ld_c, ld_wt, ld_wT, ld_s = sem("ld_c"), sem("ld_wt"), sem("ld_wT"), sem("ld_s")
    zg_done = sem("zg_done")
    z_done, zev_dve, zev_act = sem("z_done"), sem("zev_dve"), sem("zev_act")
    dve_s, act_s = sem("dve_chain"), sem("act_chain")
    ga_done, gl_done, lf_done = sem("ga_done"), sem("gl_done"), sem("lf_done")
    g_pe = sem("gate_pe")
    um_done, rr_in, rr_done, br_done, rows_in, rows_done, cols_a, cols_done, nmu_done = (
        sem(n) for n in ("um_done", "rr_in", "rr_done", "br_done", "rows_in", "rows_done", "cols_a", "cols_done", "nmu_done"))
    conv_done, silu_done = sem("conv_done"), sem("silu_done")
    wst_done, wst_ev = sem("wst_done"), sem("wst_ev")
    kt_pe, kt_ev = sem("kt_pe"), sem("kt_ev")
    kw_done, cl_done, st_done = sem("kw_done"), sem("cl_done"), sem("st_done")
    qk_done, bc_done = sem("qk_done"), sem("bc_done")
    ie_done, dm_done, ex_done, qs_done, sm_done, num_done, hs_done = (
        sem(n) for n in ("ie_done", "dm_done", "ex_done", "qs_done", "sm_done", "num_done", "hs_done"))
    hc_done, hq_done, hn_done, ht_done, ht_ev = (sem(n) for n in ("hc_done", "hq_done", "hn_done", "ht_done", "ht_ev"))
    vl_a, vl_q, vl_done, sg_done, sg_ev = (sem(n) for n in ("vl_a", "vl_q", "vl_done", "sg_done", "sg_ev"))
    bd_pe, bd_ev, pf_pe, pf_ev, dft_in, dft_used, dft_done, mix_ev, bd_zero = (
        sem(n) for n in ("bd_pe", "bd_ev", "pf_pe", "pf_ev", "dft_in", "dft_used", "dft_done", "mix_ev", "bd_zero"))
    dft_l = [sem(f"dft_l{i}") for i in range(2)]
    ready = sem("mv_ones")

    UN = units()
    on_act = {"zf", "zu", "zv", "zo"}
    ev_count = []
    a = d = 0
    for kind, _, _ in UN:
        if kind in on_act:
            a += 1
            ev_count.append((zev_act, a))
        else:
            d += 1
            ev_count.append((zev_dve, d))
    NA_UN, ND_UN = a, d
    GATE_AFTER = {u: g for g, u in enumerate(range(1, 7), 1)}

    def tok(t):
        return slice(t * P, (t + 1) * P)

    with nc.Block() as block:
        @block.sync
        def _(sp):
            sp.dma_start(cst[:, :], io["consts"]).then_inc(ld_c, 16)
            sp.dma_start(g1c[:, :], io["norm1_g"].rearrange("a (k p) -> p (a k)", p=P),
                         allow_slow_non_contiguous=True).then_inc(ld_c, 16)
            for t in range(T):
                if t >= 2:
                    sp.wait_ge(xt_done, t - 1)
                sp.dma_start(xin[:, t % 2, :], io["x"][0, tok(t), :]).then_inc(x_in[t % 2], 16)
                if t == 1:
                    w = io["w_in"].rearrange("a (k p) n -> p (a k) n", p=P)
                    sp.dma_start(wt[:, :, 256:1296], w[:, :, C_MV:C_END]).then_inc(ld_wt, 16)
            sp.dma_start(wT[:, :, 512:1024], w[:, :, C_QK:C_MV]).then_inc(ld_wT, 16)
            sp.dma_start(wT[:, :, 0:512], w[:, :, 0:C_ZV]).then_inc(ld_wT, 16)
            sp.dma_start(wt[:, :, 0:256], w[:, :, C_ZV:C_QK]).then_inc(ld_wT, 16)
            sp.wait_ge(z_done, 16)
            for t in range(T):
                if t >= 2:
                    sp.wait_ge(dft_used, t - 1)
                sp.dma_start(dft[:, t % 2, :, :], io["dft"][:, tok(t), :].rearrange("c p n -> p c n")).then_inc(dft_l[t % 2], 16)

        @block.gpsimd
        def _(pool):
            pool.memset(bd[:, :, :, :], 0.0).then_inc(bd_zero, 1)
            pool.memset(mv[:, :, :, DV:DV1], 1.0).then_inc(ready, 1)
            pool.memset(raw[:, 0:1], 0.0).then_inc(ready, 1)
            pool.memset(raw[:, S + 1:S + 2], 0.0).then_inc(ready, 1)

        @block.scalar
        def _(act):
            cwv = io["mlstm_conv_w"].rearrange("a k (c p) -> p c (a k)", p=P)
            for c in range(4):
                act.dma_start(cw[:, c, :], cwv[:, c, :], allow_slow_non_contiguous=True).then_inc(ld_s, 16)
            act.dma_start(gbr[:, :], io["mlstm_gate_b"].to_broadcast([P, 16])).then_inc(ld_s, 16)
            act.dma_start(lngb[:, 0, :], io["gmlp_ln_g"].to_broadcast([P, GW])).then_inc(ld_s, 16)
            act.dma_start(lngb[:, 1, :], io["gmlp_ln_b"].to_broadcast([P, GW])).then_inc(ld_s, 16)
            act.dma_start(gws[:, :, :], io["gmlp_ws"].rearrange("a h i j -> i (a h) j")).then_inc(ld_s, 16)
            for h in range(H):
                o = (h % 2) * 64
                act.dma_start(bsb[o:o + 64, h // 2, :], io["gmlp_bs"][0, h:h + 1, :].to_broadcast([64, P])).then_inc(ld_s, 16)
                act.dma_start(fw[o:o + 64, h // 2, :], io["four_w"][0, h, :, :]).then_inc(ld_s, 16)
            act.dma_start(ngc[:, :], io["mlstm_norm_g"].rearrange("a (h p) -> p (a h)", p=P),
                          allow_slow_non_contiguous=True).then_inc(ld_s, 16)
            for t in range(T):
                act.wait_ge(x_in[t % 2], 16 * (t // 2 + 1))
                act.activation(tmp2(zo, t), xin[:, t % 2, :], ACT.Square, accum_out=ss[:, t:t + 1]).then_inc(sq_done, 1)
                act.wait_ge(sq_done, t + 1)
                act.activation(rs[:, t:t + 1], ss[:, t:t + 1], ACT.Sqrt, bias=cst[:, K_EPS:K_EPS + 1], scale=1.0 / D).then_inc(rs_done, 1)
            act.wait_ge(ga_done, 1)
            act.activation(ga[:, :], ga[:, :], ACT.Exp).then_inc(act_s, 1)
            act.wait_ge(act_s, 1)
            act.activation(gl[:, :], ga[:, :], ACT.Ln, bias=cst[:, K_ONES:K_ONES + 1]).then_inc(gl_done, 1)
            act.wait_ge(rr_in, 1)
            act.activation(rr[0:1, 1:3, :], rr[0:1, 1:3, :], ACT.Exp).then_inc(rr_done, 1)
            act.wait_ge(rows_in, 1)
            act.activation(rows4[:, 1:3, :], rows4[:, 1:3, :], ACT.Exp).then_inc(rows_done, 1)
            for c in range(4):
                act.wait_ge(conv_done, c + 1)
                act.activation(qkT[:, c, :], qkT[:, c, :], ACT.Silu).then_inc(silu_done, 1)
            for u, (kind, c, hf) in enumerate(UN):
                if kind not in on_act:
                    continue
                act.wait_ge(z_done, u + 1)
                src = ps[:, u % 4, :]
                if kind == "zf":
                    i = act.activation(zfT[:, c, hf * 512:hf * 512 + 512], src, ACT.Copy)
                elif kind == "zu":
                    i = act.activation(uT[:, c, hf * 512:hf * 512 + 512], src, ACT.Gelu_apprx_tanh)
                elif kind == "zv":
                    i = act.activation(vg[:, c, :], src[:, 0:GW], ACT.Gelu_apprx_tanh)
                else:
                    i = act.activation(zo[:, c, :, :].rearrange("p h n -> p (h n)"), src, ACT.Sigmoid)
                i.then_inc(zev_act, 1)
            for t in range(T):
                act.wait_ge(pf_pe, t + 1)
                act.activation(pf[:, t, :], ps[:, 4 + t % 2, :], ACT.Copy).then_inc(pf_ev, 1)
            for t in range(T):
                act.wait_ge(kt_pe, t + 1)
                act.activation(kt[:, t, :], ps[:, 4 + t % 2, 0:256], ACT.Copy).then_inc(kt_ev, 1)
            for t in range(T):
                act.wait_ge(vl_a, t + 1)
                act.activation(tmp[:, 0:GW], vg[:, t, :], ACT.Square).then_inc(vl_q, 1)
            for n in range(2 * T):
                t, dr = n // 2, n % 2
                cc = t if dr == 0 else T - 1 - t
                act.wait_ge(bc_done, n + 1)
                if n:
                    act.wait_ge(qs_done, n)
                for h in range(H):
                    o = (h % 2) * 64
                    col = dr * 32 + cc * 4 + h
                    act.activation(ie[o:o + 64, h // 2, :], ps[o:o + 64, 1, h * P:(h + 1) * P], ACT.Exp,
                                   bias=br[o:o + 64, 0, col:col + 1]).then_inc(ie_done, 1)
                act.wait_ge(dm_done, n + 1)
                for h in range(H):
                    col = dr * 32 + cc * 4 + h
                    act.activation(dm[:, h, :], dm[:, h, :], ACT.Exp, bias=cols[:, 0, col:col + 1]).then_inc(ex_done, 1)
                if dr == 1:
                    act.wait_ge(hc_done, t + 1)
                    act.activation(tmp[:, :], zo[:, t, :, :].rearrange("p h n -> p (h n)"), ACT.Square).then_inc(hq_done, 1)
            act.wait_ge(vs_done, T)
            act.activation(rv[:, 0:4 * T], vs[:, 0:4 * T], ACT.Sqrt, bias=cst[:, K_EPS:K_EPS + 1], scale=1.0 / DV).then_inc(sd_done, 1)
            act.activation(rv[:, 4 * T:5 * T], vs[:, 4 * T:5 * T], ACT.Sqrt, bias=cst[:, K_EPS:K_EPS + 1], scale=1.0 / GW).then_inc(sd_done, 1)

        @block.vector
        def _(v):
            n = [0]

            def link(i):
                n[0] += 1
                i.then_inc(dve_s, 1)
                v.wait_ge(dve_s, n[0])

            v.wait_ge(ld_c, 32)
            for t in range(T):
                v.wait_ge(rs_done, t + 1)
                link(v.reciprocal(rs[:, t:t + 1], rs[:, t:t + 1]))
                v.tensor_scalar(xin[:, t % 2, :], xin[:, t % 2, :], rs[:, t:t + 1], None, ALU.mult).then_inc(xs_done, 1)
                for b in range(2):
                    v.wait_ge(xt_done, t + 1)
                    v.tensor_tensor(aT[:, b * 4:b * 4 + 4, tok(t)],
                                    ps[:, 2 * (t % 2) + b, :].rearrange("p (k n) -> p k n", k=4),
                                    g1c[:, b * 4:b * 4 + 4, None].to_broadcast([P, 4, P]), ALU.mult).then_inc(at_done, 1)
            v.wait_ge(ld_s, 16 * 17)
            v.wait_ge(zg_done, 1)
            pg = ps[:, 4, 0:128].rearrange("p (d c g) -> p d c g", d=2, c=T)
            g4 = lambda x: x.rearrange("p (d c h) -> p d c h", d=2, c=T)
            gb4 = gbr[:, :].rearrange("p (d g) -> p d g", d=2)
            for dr in range(2):
                v.tensor_tensor(g4(gi[:, :])[:, dr], pg[:, dr, :, 0:4], gb4[:, dr, None, 0:4].to_broadcast([P, T, 4]), ALU.add).then_inc(dve_s, 1)
                v.tensor_tensor(g4(gf[:, :])[:, dr], pg[:, dr, :, 4:8], gb4[:, dr, None, 4:8].to_broadcast([P, T, 4]), ALU.add).then_inc(dve_s, 1)
                n[0] += 2
            v.wait_ge(dve_s, n[0])
            v.scalar_tensor_tensor(ga[:, :], gf[:, :], -1.0, gf[:, :], ALU.mult, ALU.min).then_inc(ga_done, 1)
            v.wait_ge(gl_done, 1)
            v.scalar_tensor_tensor(gf[:, :], gf[:, :], 0.0, gl[:, :], ALU.min, ALU.subtract).then_inc(lf_done, 1)

            def gate_step(g):
                v.wait_ge(g_pe, g)
                if g == 1:
                    link(v.tensor_copy(rowb[:, :], ps[0:64, 5, 0:P]))
                    link(v.tensor_tensor(rowu[:, :], ps[0:64, 5, P:2 * P], rowb[:, :], ALU.subtract))
                    link(v.tensor_tensor_scan(cumx[:, :], rowu[:, :], rowu[:, :], -3.0e38, ALU.max, ALU.max))
                    v.tensor_copy(um[:, 0:1], cumx[:, P - 1:P]).then_inc(um_done, 1)
                    v.tensor_copy(um[:, 1:2], rowb[:, P - 1:P]).then_inc(um_done, 1)
                elif g == 2:
                    link(v.memset(rm[:, :, :, :], 0.0))
                    link(v.tensor_copy(r1[0:1, :, :].rearrange("p a n -> p (a n)"), ps[0:1, 6, 0:128]))
                    r4 = r1[0:1, :, :].rearrange("p a (d c h) -> p a d c h", d=2, c=T)
                    for dr in range(2):
                        for h in range(H):
                            link(v.tensor_tensor_scan(rm[0:1, dr, 1:9, h], r4[0:1, 0, dr, :, h], r4[0:1, 1, dr, :, h], 0.0, ALU.max, ALU.add))
                    rr4 = rr[0:1, :, :].rearrange("p a (d c h) -> p a d c h", d=2, c=T)
                    link(v.tensor_copy(rr4[0:1, 0], rm[0:1, :, 0:8, :]))
                    link(v.tensor_tensor(mx[:, :], rr[0:1, 0, :], r1[0:1, 0, :], ALU.max))
                    link(v.tensor_tensor(rr[0:1, 1, :], rr[0:1, 0, :], mx[:, :], ALU.subtract))
                    v.tensor_tensor(rr[0:1, 2, :], r1[0:1, 0, :], mx[:, :], ALU.subtract).then_inc(rr_in, 1)
                elif g == 3:
                    link(v.tensor_copy(br[:, :, :].rearrange("p a n -> p (a n)"), ps[:, 5, 0:192]))
                    link(v.tensor_copy(mpc[:, :], ps[0:64, 5, 256:257]))
                    for hf in range(2):
                        s4 = br[hf * 64:hf * 64 + 64, 1:3, :].rearrange("p a (n q e) -> p a n q e", q=2, e=2)
                        v.tensor_copy(ao[hf * 64:hf * 64 + 64, :, :, :].rearrange("p a q n -> p a n q"), s4[:, :, :, :, hf]).then_inc(br_done, 1)
                    link(v.tensor_scalar(cumx[:, :], cumx[:, :], mpc[:, :], None, ALU.max))
                    link(v.tensor_scalar(rows4[:, 3, :], cumx[:, :], -1.0, None, ALU.mult))
                    link(v.tensor_copy(rows4[:, 0, :], rowu[:, :]))
                    link(v.tensor_scalar(rows4[:, 1, :], rowu[:, :], um[:, 0:1], None, ALU.subtract))
                    v.tensor_tensor(rows4[:, 2, :], rows4[:, 3, :], rowb[:, :], ALU.subtract).then_inc(rows_in, 1)
                elif g == 4:
                    v.tensor_copy(cols[:, :, :].rearrange("p a n -> p (a n)"), ps[:, 6, 0:256]).then_inc(cols_a, 1)
                elif g == 5:
                    v.tensor_copy(cols[:, :, 32:64], ps[:, 5, 0:128].rearrange("p (a n) -> p a n", a=4)).then_inc(cols_done, 1)
                else:
                    v.tensor_copy(nmu[:, :], ps[0:64, 6, 0:P]).then_inc(nmu_done, 1)

            def evacuate(u):
                kind, c, hf = UN[u]
                v.wait_ge(z_done, u + 1)
                src = ps[:, u % 4, :]
                if kind == "qk":
                    if u >= 2:
                        v.wait_ge(conv_done, c)
                    else:
                        v.wait_ge(ready, 3)
                    link(v.tensor_copy(raw[:, 1 + hf * 512:513 + hf * 512], src))
                    v.sem_inc(zev_dve, 1)
                    if hf == 1:
                        link(v.tensor_scalar(qkT[:, c, :], raw[:, 0:S], cw[:, c, 0:1], None, ALU.mult))
                        link(v.scalar_tensor_tensor(qkT[:, c, :], raw[:, 1:S + 1], cw[:, c, 1:2], qkT[:, c, :], ALU.mult, ALU.add))
                        v.scalar_tensor_tensor(qkT[:, c, :], raw[:, 2:S + 2], cw[:, c, 2:3], qkT[:, c, :], ALU.mult, ALU.add).then_inc(conv_done, 1)
                else:
                    v.tensor_copy(mv[:, c, :, 0:DV], src.rearrange("p (h n) -> p h n", h=H)).then_inc(zev_dve, 1)

            for u, (kind, _, _) in enumerate(UN):
                if kind not in on_act:
                    evacuate(u)
                if u in GATE_AFTER:
                    gate_step(GATE_AFTER[u])
                if u == 9:
                    v.wait_ge(wst_done, 1)
                    v.tensor_copy(wsT[:, :, :].rearrange("p h n -> p (h n)"), ps[:, 7, :]).then_inc(wst_ev, 1)
                    v.wait_ge(bd_pe, 1)
                    v.wait_ge(bd_zero, 1)
                    for h in range(H):
                        o = (h % 2) * 64
                        v.tensor_copy(bd[o:o + 64, :, h // 2, o:o + 64],
                                      ps[o:o + 64, 6, :].rearrange("p (c q n) -> p c q n", c=2, q=4)[:, :, h // 2, 0:64]).then_inc(bd_ev, 1)
            v.wait_ge(silu_done, 4)
            for c in range(2):
                link(v.tensor_scalar(qkT[:, c, :], qkT[:, c, :], DK ** -0.5, None, ALU.mult))
            v.wait_ge(zev_act, NA_UN)
            for t in range(T):
                link(v.tensor_reduce(st4[:, 0, 0:1], vg[:, t, :], AX.X, ALU.add))
                link(v.tensor_scalar(st4[:, 0, 0:1], st4[:, 0, 0:1], 1.0 / GW, None, ALU.mult))
                v.tensor_scalar(vg[:, t, :], vg[:, t, :], st4[:, 0, 0:1], None, ALU.subtract).then_inc(vl_a, 1)
                v.wait_ge(vl_q, t + 1)
                link(v.tensor_reduce(vs[:, 4 * T + t:4 * T + t + 1], tmp[:, 0:GW], AX.X, ALU.add))
            for c in range(T):
                for dr in range(2):
                    m = 2 * c + dr
                    t = c if dr == 0 else T - 1 - c
                    n0 = dr * 32 + c * 4
                    if c == 0 and dr == 0:
                        v.wait_ge(zev_act, NA_UN)
                        v.wait_ge(z_done, len(UN))
                        link(v.memset(st[:, :, :, 0, :], 0.0))
                        v.wait_ge(kt_ev, T)
                    if c == T - 1:
                        continue
                    if m >= 2:
                        v.wait_ge(cl_done, m - 1)
                    v.tensor_tensor(kw[:, m % 2, :].rearrange("p (h n) -> p h n", h=H),
                                    kt[:, t, :].rearrange("p (h n) -> p h n", h=H),
                                    cols[:, 1, n0:n0 + 4, None].to_broadcast([P, 4, DK]), ALU.mult).then_inc(kw_done, 1)
                    v.wait_ge(cl_done, m + 1)
                    for q in range(2):
                        link(v.tensor_scalar(tmp[:, 0:DV1], ps[:, 6 + m % 2, q * DV1:q * DV1 + DV1],
                                             ao[:, 1, q, dr * 8 + c:dr * 8 + c + 1], None, ALU.mult))
                        link(v.scalar_tensor_tensor(st[:, q, dr, c + 1, :], st[:, q, dr, c, :],
                                                    ao[:, 0, q, dr * 8 + c:dr * 8 + c + 1], tmp[:, 0:DV1], ALU.mult, ALU.add))
                    v.sem_inc(st_done, 1)
            for m in range(2 * T):
                t, dr = m // 2, m % 2
                cc = t if dr == 0 else T - 1 - t
                n0 = dr * 32 + cc * 4
                v.wait_ge(bc_done, m + 1)
                v.wait_ge(ie_done, 4 * (m + 1))
                neg = K_NEGF if dr == 0 else K_NEGB
                v.tensor_tensor(dm[:, :, :], ps[:, 1, :].rearrange("p (h n) -> p h n", h=H),
                                cst[:, None, neg:neg + P].to_broadcast([P, 4, P]), ALU.add).then_inc(dm_done, 1)
                if m >= 2:
                    v.wait_ge(num_done, m - 1)
                v.tensor_tensor(qs[:, m % 2, :, :], qkT[:, 0:2, tok(t)], ie[:, :, :], ALU.mult).then_inc(qs_done, 1)
                v.wait_ge(ex_done, 4 * (m + 1))
                v.wait_ge(qk_done, t + 1)
                v.tensor_tensor(sm[:, m % 2, :, :].rearrange("p (q e) n -> p e q n", q=2),
                                ps[:, 6:8, 0:256].rearrange("p e (q n) -> p e q n", q=2),
                                dm[:, :, :].rearrange("p (q e) n -> p e q n", q=2), ALU.mult).then_inc(sm_done, 1)
                v.wait_ge(num_done, m + 1)
                pn = ps[:, 2 + 2 * (m % 2):4 + 2 * (m % 2), :].rearrange("p e (q n) -> p e q n", q=2)
                dn = den[:, dr, :].rearrange("p (q e) -> p e q", q=2)
                cl = cols[:, 2, n0:n0 + 4].rearrange("p (q e) -> p e q", q=2)
                link(v.scalar_tensor_tensor(dn, pn[:, :, :, DV], -1.0, cl, ALU.mult, ALU.max))
                link(v.tensor_tensor(dn, pn[:, :, :, DV], dn, ALU.max))
                link(v.reciprocal(den[:, dr, :], den[:, dr, :]))
                rb = dn[:, :, :, None].to_broadcast([P, 2, 2, DV])
                hv = hm[:, :, :].rearrange("p (q e) n -> p e q n", q=2)
                if dr == 0:
                    link(v.tensor_tensor(hv, pn[:, :, :, 0:DV], rb, ALU.mult))
                    v.sem_inc(hs_done, 1)
                    continue
                tv = tmp[:, :].rearrange("p (q e n) -> p e q n", q=2, e=2)
                link(v.tensor_tensor(tv, pn[:, :, :, 0:DV], rb, ALU.mult))
                v.sem_inc(hs_done, 1)
                t4 = tmp[:, :].rearrange("p (h n) -> p h n", h=H)
                link(v.tensor_tensor(hm[:, :, :], hm[:, :, :], t4, ALU.add))
                link(v.tensor_tensor(zo[:, t, :, :], hm[:, :, :], zo[:, t, :, :], ALU.mult))
                link(v.tensor_reduce(st4[:, 0, :], zo[:, t, :, :], AX.X, ALU.add))
                link(v.tensor_scalar(st4[:, 0, :], st4[:, 0, :], 1.0 / DV, None, ALU.mult))
                link(v.tensor_tensor(zo[:, t, :, :], zo[:, t, :, :], st4[:, 0, :, None].to_broadcast([P, H, DV]), ALU.subtract))
                v.sem_inc(hc_done, 1)
                v.wait_ge(hq_done, t + 1)
                link(v.tensor_reduce(vs[:, 4 * t:4 * t + 4], t4, AX.X, ALU.add))
                v.sem_inc(vs_done, 1)
            v.wait_ge(sd_done, 2)
            link(v.reciprocal(rv[:, :], rv[:, :]))
            for t in range(T):
                if t >= 2:
                    v.wait_ge(ht_done, t - 1)
                v.tensor_tensor(hn[:, t % 2, :, :], zo[:, t, :, :], rv[:, 4 * t:4 * t + 4, None].to_broadcast([P, H, DV]), ALU.mult).then_inc(hn_done, 1)
                link(v.scalar_tensor_tensor(vg[:, t, :], vg[:, t, :], rv[:, 4 * T + t:4 * T + t + 1], lngb[:, 0, :], ALU.mult, ALU.mult))
                v.tensor_tensor(vg[:, t, :], vg[:, t, :], lngb[:, 1, :], ALU.add).then_inc(vl_done, 1)
                v.wait_ge(ht_done, t + 1)
                v.tensor_tensor(mixT[:, 4:8, tok(t)], ps[:, 6, :].rearrange("p (h n) -> p h n", h=H),
                                ngc[:, :, None].to_broadcast([P, H, P]), ALU.mult).then_inc(ht_ev, 1)
                v.wait_ge(sg_done, t + 1)
                tq = tmp[:, 256:512].rearrange("p (q n) -> p q n", q=2)
                link(v.tensor_tensor(tq, ps[:, 7, 0:256].rearrange("p (q n) -> p q n", q=2), bsb[:, :, :], ALU.add))
                v.tensor_tensor(mixT[:, 2:4, tok(t)], tq, uT[:, :, tok(t)], ALU.mult).then_inc(sg_ev, 1)
            for q in range(2):
                for hf in range(2):
                    v.wait_ge(dft_used, T)
                    v.tensor_copy(mixT[:, q, hf * 512:hf * 512 + 512], ps[:, 2 * q + hf, :]).then_inc(mix_ev, 1)
            v.wait_ge(mix_ev, 4)

        @block.tensor
        def _(pe):
            mm = nc.tensor.matmul
            pe.wait_ge(ld_c, 32)
            for t in range(T):
                pe.wait_ge(xs_done, t + 1)
                if t >= 2:
                    pe.wait_ge(at_done, 2 * (t - 1))
                for k in range(KD):
                    i = nc.tensor.transpose(ps[:, 2 * (t % 2) + k // 4, (k % 4) * P:(k % 4 + 1) * P], xin[:, t % 2, k * P:(k + 1) * P], ident)
                i.then_inc(xt_done, 1)
                if t >= 1:
                    gates_of(pe, mm, t - 1, aT, wt, ps, at_done, ld_wt)
            i = gates_of(pe, mm, T - 1, aT, wt, ps, at_done, ld_wt)
            i.then_inc(zg_done, 1)

            def gate_step(g):
                if g == 1:
                    pe.wait_ge(lf_done, 1)
                    mm(ps[0:32, 5, 0:P], gf[:, 0:32], cst[:, K_UP:K_UP + P], start=True, stop=True)
                    mm(ps[32:64, 5, 0:P], gf[:, 32:64], cst[:, K_REVUP:K_REVUP + P], start=True, stop=True)
                    mm(ps[0:32, 5, P:2 * P], gi[:, 0:32], ident, start=True, stop=True)
                    i = mm(ps[32:64, 5, P:2 * P], gi[:, 32:64], rev, start=True, stop=True)
                elif g == 2:
                    pe.wait_ge(um_done, 2)
                    for j in range(2):
                        i = mm(ps[0:1, 6, j * 64:j * 64 + 64], um[:, j:j + 1], ident[0:64, 0:64], start=True, stop=True)
                elif g == 3:
                    pe.wait_ge(rr_done, 1)
                    mm(ps[:, 5, 0:192], cst[0:1, K_ONES:K_ONES + P], rr[0:1, :, :].rearrange("p a n -> p (a n)"), start=True, stop=True)
                    i = mm(ps[0:64, 5, 256:257], rr[0:1, 0, :], cst[0:1, K_ONES:K_ONES + 1], start=True, stop=True)
                elif g == 4:
                    pe.wait_ge(rows_done, 1)
                    for j in range(4):
                        i = mm(ps[:, 6, j * 64:j * 64 + 64], rows4[:, j, :], ident[0:64, 0:64], start=True, stop=True)
                elif g == 5:
                    pe.wait_ge(cols_a, 1)
                    i = mm(ps[:, 5, 0:128].rearrange("p (a n) -> p a n", a=4), rev, cols[:, :, 32:64], start=True, stop=True)
                else:
                    pe.wait_ge(cols_done, 1)
                    i = mm(ps[0:64, 6, 0:P], cols[:, 3, :], ident, start=True, stop=True)
                i.then_inc(g_pe, 1)

            pe.wait_ge(at_done, 2 * T)
            for u, (kind, c, hf) in enumerate(UN):
                if u >= 4:
                    pe.wait_ge(*ev_count[u - 4])
                if u == 0:
                    pe.wait_ge(ld_wT, 48)
                for k in range(KD):
                    if kind in ("qk", "zf", "zu"):
                        o = {"zf": 0, "zu": 256, "qk": 512}[kind] + c * P
                        i = mm(ps[:, u % 4, :], wT[:, k, o:o + P], aT[:, k, hf * 512:hf * 512 + 512], start=k == 0, stop=k == KD - 1)
                    else:
                        o, w = {"zv": (0, 256), "mv": (256, 512), "zo": (768, 512)}[kind]
                        i = mm(ps[:, u % 4, 0:w], aT[:, k, tok(c)], wt[:, k, o:o + w], start=k == 0, stop=k == KD - 1)
                i.then_inc(z_done, 1)
                if u in GATE_AFTER:
                    gate_step(GATE_AFTER[u])
                if u == 8:
                    pe.wait_ge(ld_s, 16 * 17)
                    for h in range(H):
                        i = nc.tensor.transpose(ps[:, 7, h * P:(h + 1) * P], gws[:, h, :], ident)
                    i.then_inc(wst_done, 1)
                    pe.wait_ge(nmu_done, 1)
                    for h in range(H):
                        o = (h % 2) * 64
                        for c2 in range(2):
                            at = c2 * 256 + (h // 2) * 64
                            i = mm(ps[o:o + 64, 6, at:at + 64], cst[o:o + 64, (K_DC, K_DS)[c2]:(K_DC, K_DS)[c2] + 64], fw[o:o + 64, h // 2, :], start=True, stop=True)
                    i.then_inc(bd_pe, 1)
            pe.wait_ge(bd_ev, 4)
            pe.wait_ge(zev_act, NA_UN)
            pe.wait_ge(zev_dve, ND_UN)
            for t in range(T):
                if t >= 2:
                    pe.wait_ge(pf_ev, t - 1)
                for c2 in range(2):
                    for q in range(2):
                        i = mm(ps[:, 4 + t % 2, c2 * 256 + q * P:c2 * 256 + q * P + P], zfT[:, q, tok(t)], bd[:, c2, q, :], start=True, stop=True)
                i.then_inc(pf_pe, 1)
            pe.wait_ge(silu_done, 4)
            pe.wait_ge(pf_ev, T)
            for t in range(T):
                if t >= 2:
                    pe.wait_ge(kt_ev, t - 1)
                for q in range(2):
                    i = nc.tensor.transpose(ps[:, 4 + t % 2, q * P:(q + 1) * P], qkT[:, 2 + q, tok(t)], ident)
                i.then_inc(kt_pe, 1)
            for c in range(T - 1):
                for dr in range(2):
                    m = 2 * c + dr
                    t = c if dr == 0 else T - 1 - c
                    pe.wait_ge(kw_done, m + 1)
                    if m >= 2:
                        pe.wait_ge(st_done, m - 1)
                    for h in range(H):
                        o = (h % 2) * 64
                        i = mm(ps[o:o + 64, 6 + m % 2, (h // 2) * DV1:(h // 2) * DV1 + DV1], kw[:, m % 2, h * DK:(h + 1) * DK], mv[:, t, h, :], start=True, stop=True)
                    i.then_inc(cl_done, 1)
            pe.wait_ge(st_done, 2 * (T - 1))

            def scores(m):
                t, dr = m // 2, m % 2
                cc = t if dr == 0 else T - 1 - t
                if dr == 0:
                    if m:
                        pe.wait_ge(sm_done, m)
                    for h in range(H):
                        o = (h % 2) * 64
                        i = mm(ps[:, 6 + h % 2, (h // 2) * P:(h // 2 + 1) * P], qkT[o:o + 64, 2 + h // 2, tok(t)], qkT[o:o + 64, h // 2, tok(t)], start=True, stop=True)
                    i.then_inc(qk_done, 1)
                if m:
                    pe.wait_ge(dm_done, m)
                for h in range(H):
                    col = dr * 32 + cc * 4 + h
                    i = mm(ps[:, 1, h * P:(h + 1) * P], ident[0:64, col:col + 1].to_broadcast([64, P]), nmu[:, :], start=True, stop=True)
                i.then_inc(bc_done, 1)

            scores(0)
            for m in range(2 * T):
                t, dr = m // 2, m % 2
                cc = t if dr == 0 else T - 1 - t
                if m + 1 < 2 * T and dr == 0:
                    scores(m + 1)
                pe.wait_ge(sm_done, m + 1)
                if m >= 2:
                    pe.wait_ge(hs_done, m - 1)
                for h in range(H):
                    o = (h % 2) * 64
                    dst = ps[:, 2 + 2 * (m % 2) + h % 2, (h // 2) * 256:(h // 2) * 256 + DV1]
                    mm(dst, sm[:, m % 2, h, :], mv[:, t, h, :], start=True, stop=False)
                    i = mm(dst, qs[o:o + 64, m % 2, h // 2, :], st[o:o + 64, h // 2, dr, cc, :], start=False, stop=True)
                i.then_inc(num_done, 1)
                if dr == 1:
                    if m + 1 < 2 * T:
                        scores(m + 1)
            pe.wait_ge(hs_done, 2 * T)
            for t in range(T):
                pe.wait_ge(hn_done, t + 1)
                if t:
                    pe.wait_ge(ht_ev, t)
                for h in range(H):
                    i = nc.tensor.transpose(ps[:, 6, h * P:(h + 1) * P], hn[:, t % 2, h, :], ident)
                i.then_inc(ht_done, 1)
                pe.wait_ge(vl_done, t + 1)
                if t:
                    pe.wait_ge(sg_ev, t)
                for h in range(H):
                    o = (h % 2) * 64
                    i = mm(ps[o:o + 64, 7, (h // 2) * P:(h // 2) * P + P], vg[:, t, h * 64:h * 64 + 64], wsT[:, h, :], start=True, stop=True)
                i.then_inc(sg_done, 1)
            pe.wait_ge(hs_done, 2 * T)
            pe.wait_ge(sm_done, 2 * T)
            for t in range(T):
                pe.wait_ge(dft_l[t % 2], 16 * (t // 2 + 1))
                for q in range(2):
                    for hf in range(2):
                        for c2 in range(2):
                            i = mm(ps[:, 2 * q + hf, :], pf[:, t, c2 * 256 + q * P:c2 * 256 + q * P + P], dft[:, t % 2, c2, hf * 512:hf * 512 + 512],
                                   start=t == 0 and c2 == 0, stop=t == T - 1 and c2 == 1)
                i.then_inc(dft_used, 1)
    return ps


def tmp2(zo, t):
    return zo[:, 2 * (t % 4):2 * (t % 4) + 2, :, :].rearrange("p a h n -> p (a h n)")


def gates_of(pe, mm, t, aT, wt, ps, at_done, ld_wt):
    pe.wait_ge(at_done, 2 * (t + 1))
    pe.wait_ge(ld_wt, 16)
    for dr in range(2):
        at = (t if dr == 0 else 8 + T - 1 - t) * 8
        for k in range(KD):
            i = mm(ps[:, 4, at:at + 8], aT[:, k, t * P:(t + 1) * P], wt[:, k, 1280 + dr * 8:1288 + dr * 8], start=k == 0, stop=k == KD - 1)
    return i


def route(nc, ctx, io, cst, mixT, tab):
    def sb(name, shape, dt=F32):
        return ctx.enter_context(nc.sbuf_tensor(name, shape, dt))

    def sem(name):
        return ctx.enter_context(nc.semaphore(name))

    ident = cst[:, K_ID:K_ID + P]
    strict = cst[:, K_STRICT:K_STRICT + P]
    ones = cst[:, K_ONES:K_ONES + P]
    iota = cst[:, K_IOTA:K_IOTA + NI]
    xmT = mixT
    wo = sb("wo", [P, KD, D])
    hh = sb("hh", [P, T, D])
    rw = sb("rw", [P, KD, NE])
    sgu = sb("sgu", [P, KD, 2 * DE])
    sd = sb("sd", [P, 2, D])
    g2b = sb("g2b", [P, D])
    rbb = sb("rbb", [P, NE])
    xt = sb("xt", [P, 2, D])
    xm = sb("xm", [P, 2, D])
    ss, rs = sb("ss2", [P, T]), sb("rs2", [P, T])
    ex = sb("ex", [P, 2, NE])
    vv = sb("vv", [P, NE])
    mr = sb("mr", [P, NE])
    m8 = sb("m8", [P, 8])
    gs = sb("gs", [P, 1])
    M, G, V = sb("M", [P, T, NE]), sb("G", [P, T, NE]), sb("V", [P, T, NE])
    V8, g8 = sb("V8", [P, 64]), sb("g8", [P, 64])
    it32, itf, pf8 = sb("it32", [P, 64], I32), sb("itf", [P, 64]), sb("pf8", [P, 64])
    cnt = sb("cnt", [P, 1])
    t8 = sb("t8", [P, 8])
    nba = sb("nba", [P, 2])
    bo = sb("bo", [P, 2])
    ec = sb("ec", [P, 8])
    t43 = sb("t43", [P, 64])
    R = sb("R", [P, NE])
    ind = sb("ind", [P, NI])
    ind2 = sb("ind2", [P, NE])
    A = sb("A", [P, 2, P])
    B = sb("B", [P, 2, 2 * NI])
    e0 = sb("e0", [P, NI])
    sg = sb("sg", [P, DE])
    hx = sb("hx", [P, DE])
    hT = sb("hT", [P, 2, P])
    ps = ctx.enter_context(nc.psum_tensor("ps_route", [P, 8, 512], F32))

    ld_w, ld_s, ld_sh = sem("r_ld_w"), sem("r_ld_s"), sem("r_ld_sh")
    x_in = [sem(f"r_x{i}") for i in range(2)]
    h_pe, h_done, sq_done, sd_done, xm_done = (sem(n) for n in ("h_pe", "h_done", "r_sq", "r_sd", "xm_done"))
    xm_st = [sem(f"xm_st{i}") for i in range(2)]
    xt_pe, xt_ev, lg_pe, ex_done, chain = (sem(n) for n in ("xt_pe", "xt_ev", "lg_pe", "r_ex", "r_chain"))
    m_done, cnt_pe, nba_done, bo_pe, cols_done, rows_pe, rows_ev, v_pe, v_done = (
        sem(n) for n in ("m_done", "cnt_pe", "nba_done", "bo_pe", "r_cols", "rows_pe", "rows_ev", "v_pe", "v_done"))
    ab_done, ab_used = sem("ab_done"), sem("ab_used")
    gu_pe, sg_done, hx_done, ht_pe, ht_ev, dn_pe, acc_in = (
        sem(n) for n in ("gu_pe", "r_sg", "hx_done", "r_ht_pe", "r_ht_ev", "dn_pe", "acc_in"))
    acc_st = sem("acc_st")

    def tok(t):
        return slice(t * P, (t + 1) * P)

    with nc.Block() as block:
        @block.sync
        def _(sp):
            wv = io["w_out"].rearrange("a (k p) n -> p (a k) n", p=P)
            sp.dma_start(wo[:, :, 0:512], wv[:, :, 0:512]).then_inc(ld_w, 16)
            sp.dma_start(wo[:, :, 512:1024], wv[:, :, 512:1024]).then_inc(ld_w, 16)
            for t in range(2):
                sp.dma_start(xt[:, t, :], io["x"][0, tok(t), :]).then_inc(x_in[t], 16)
            sp.dma_start(rw[:, :, :], io["router_w"].rearrange("a (k p) n -> p (a k) n", p=P)).then_inc(ld_s, 16)
            sp.dma_start(sgu[:, :, 0:DE], io["sh_w_gate"].rearrange("a (k p) n -> p (a k) n", p=P)).then_inc(ld_sh, 16)
            sp.dma_start(sgu[:, :, DE:2 * DE], io["sh_w_up"].rearrange("a (k p) n -> p (a k) n", p=P)).then_inc(ld_sh, 16)
            sp.dma_start(sd[:, :, :], io["sh_w_down"].rearrange("a (j p) n -> p (a j) n", p=P)).then_inc(ld_sh, 16)
            for t in range(T):
                sp.wait_ge(xm_done, t + 1)
                sp.dma_start(io["xm"][tok(t), :], xm[:, t % 2, :]).then_inc(xm_st[t % 2], 16)
                if t + 2 < T:
                    sp.dma_start(xt[:, t % 2, :], io["x"][0, tok(t + 2), :]).then_inc(x_in[t % 2], 16)
            for t in range(T):
                sp.wait_ge(acc_in, t + 1)
                sp.dma_start(io["acc"][tok(t), :], hh[:, t, :]).then_inc(acc_st, 16)
            sp.wait_ge(acc_st, 16 * T)
            for b in range(2):
                sp.wait_ge(xm_st[b], 16 * (T // 2))

        @block.scalar
        def _(act):
            act.dma_start(g2b[:, :], io["norm2_g"].to_broadcast([P, D])).then_inc(ld_s, 16)
            act.dma_start(rbb[:, :], io["router_b"].to_broadcast([P, NE])).then_inc(ld_s, 16)
            for t in range(T + 1):
                if t < T:
                    act.wait_ge(h_done, t + 1)
                    if t >= 2:
                        act.wait_ge(xm_st[t % 2], 16 * (t // 2))
                    act.activation(xm[:, t % 2, :], hh[:, t, :], ACT.Square, accum_out=ss[:, t:t + 1]).then_inc(sq_done, 1)
                    act.wait_ge(sq_done, t + 1)
                    act.activation(rs[:, t:t + 1], ss[:, t:t + 1], ACT.Sqrt, bias=cst[:, K_EPS:K_EPS + 1], scale=1.0 / D).then_inc(sd_done, 1)
                    for b in range(2):
                        act.wait_ge(xt_pe, 2 * t + b + 1)
                        act.activation(xmT[:, b * 4:b * 4 + 4, tok(t)], ps[:, 4 + b, :].rearrange("p (k n) -> p k n", k=4), ACT.Copy).then_inc(xt_ev, 1)
                if t >= 1:
                    act.wait_ge(lg_pe, t)
                    if t >= 3:
                        act.wait_ge(m_done, t - 2)
                    act.activation(ex[:, (t - 1) % 2, :], ps[:, 6 + (t - 1) % 2, 0:NE], ACT.Exp, scale=-1.0).then_inc(ex_done, 1)
            for t in range(T):
                act.wait_ge(gu_pe, t + 1)
                if t:
                    act.wait_ge(hx_done, t)
                act.activation(sg[:, :], ps[:, t % 2, 0:DE], ACT.Silu).then_inc(sg_done, 1)
                act.wait_ge(ht_pe, t + 1)
                if t:
                    act.wait_ge(dn_pe, t)
                act.activation(hT[:, :, :].rearrange("p a n -> p (a n)"), ps[:, 2, 0:256], ACT.Copy).then_inc(ht_ev, 1)

        @block.vector
        def _(v):
            n = [0]

            def link(i):
                n[0] += 1
                i.then_inc(chain, 1)
                v.wait_ge(chain, n[0])

            def residual(t):
                v.wait_ge(x_in[t % 2], 16 * (t // 2 + 1))
                v.wait_ge(h_pe, t + 1)
                b = 2 * (t % 2)
                v.tensor_tensor(hh[:, t, :], ps[:, b:b + 2, :].rearrange("p a n -> p (a n)"), xt[:, t % 2, :], ALU.add).then_inc(h_done, 1)

            def norm(t):
                v.wait_ge(sd_done, t + 1)
                if t == 0:
                    v.wait_ge(ld_s, 48)
                link(v.reciprocal(rs[:, t:t + 1], rs[:, t:t + 1]))
                v.scalar_tensor_tensor(xm[:, t % 2, :], hh[:, t, :], rs[:, t:t + 1], g2b[:, :], ALU.mult, ALU.mult).then_inc(xm_done, 1)

            def choose(t):
                v.wait_ge(ex_done, t + 1)
                e = ex[:, t % 2, :]
                link(v.tensor_scalar(e, e, 1.0, None, ALU.add))
                link(v.reciprocal(e, e))
                link(v.tensor_tensor(vv[:, :], e, rbb[:, :], ALU.add))
                link(v.max(m8[:, :], vv[:, :]))
                link(v.match_replace(mr[:, :], m8[:, :], vv[:, :], -3.0e38))
                link(v.tensor_tensor(M[:, t, :], vv[:, :], mr[:, :], ALU.not_equal))
                link(v.tensor_tensor(G[:, t, :], e, M[:, t, :], ALU.mult))
                link(v.tensor_reduce(gs[:, :], G[:, t, :], AX.X, ALU.add))
                link(v.reciprocal(gs[:, :], gs[:, :]))
                v.tensor_scalar(G[:, t, :], G[:, t, :], gs[:, :], None, ALU.mult).then_inc(m_done, 1)

            residual(0)
            for t in range(T):
                if t + 1 < T:
                    residual(t + 1)
                norm(t)
                if t:
                    choose(t - 1)
            choose(T - 1)
            v.wait_ge(m_done, T)
            v.wait_ge(cnt_pe, 1)
            link(v.tensor_copy(cnt[:, :], ps[:, 7, 0:1]))
            link(v.tensor_scalar(t8[:, :], cst[:, K_T128:K_T128 + 8], cnt[:, :], None, ALU.is_lt))
            link(v.tensor_reduce(nba[:, 0:1], t8[:, :], AX.X, ALU.add))
            v.tensor_scalar(nba[:, 1:2], nba[:, 0:1], 0.0, None, ALU.is_gt).then_inc(nba_done, 1)
            v.wait_ge(bo_pe, 1)
            link(v.tensor_copy(bo[:, :], ps[:, 7, 4:6]))
            link(v.tensor_tensor(ec[:, 0:1], bo[:, 0:1], nba[:, 0:1], ALU.add))
            link(v.tensor_scalar(ec[:, 1:2], bo[:, 0:1], float(P), 1.0, ALU.mult, ALU.add))
            v.tensor_scalar(R[:, :], ident, ec[:, 1:2], None, ALU.mult).then_inc(cols_done, 1)
            link(v.tensor_scalar(t43[:, 0:42], iota[:, 1:43], float(NW), bo[:, 1:2], ALU.mult, ALU.is_le))
            link(v.tensor_reduce(ec[:, 2:3], t43[:, 0:42], AX.X, ALU.add))
            link(v.scalar_tensor_tensor(ec[:, 3:4], ec[:, 2:3], -float(NW), bo[:, 1:2], ALU.mult, ALU.add))
            link(v.tensor_scalar(ec[:, 4:5], ec[:, 2:3], 48.0, 48.0, ALU.mult, ALU.add))
            link(v.tensor_scalar(ec[:, 5:6], bo[:, 0:1], 1.0, None, ALU.add))
            link(v.tensor_scalar(e0[:, :], iota, bo[:, 0:1], None, ALU.is_ge))
            link(v.scalar_tensor_tensor(ind[:, :], iota, ec[:, 0:1], e0[:, :], ALU.is_lt, ALU.mult))
            v.tensor_scalar(ind2[:, :], iota[:, 0:NE], bo[:, 1:2], nba[:, 1:2], ALU.is_equal, ALU.mult).then_inc(cols_done, 1)
            v.wait_ge(v_pe, 1)
            link(v.tensor_tensor(V[:, :, :].rearrange("p t n -> p (t n)"), ps[:, 4:6, :].rearrange("p a n -> p (a n)"),
                                 M[:, :, :].rearrange("p t n -> p (t n)"), ALU.mult))
            v.sem_inc(v_done, 1)
            for t in range(T):
                link(v.max(V8[:, t * 8:t * 8 + 8], V[:, t, :]))
            v.wait_ge(rows_pe, 1)
            v.tensor_copy(tab["item"][0:1, 0:NI, :], ps[0:1, 7, 8:8 + 2 * NI].rearrange("p (a n) -> p n a", a=2)).then_inc(rows_ev, 1)
            v.tensor_copy(tab["expert"][0:1, 0:NE], ps[0:1, 6, 0:NE]).then_inc(rows_ev, 1)
            link(v.memset(tab["free"][0:1, 0:NW], 1))
            v.tensor_copy(tab["free"][0:1, NW:NE], ps[0:1, 6, NE + NW - 2:2 * NE - 2]).then_inc(rows_ev, 1)
            v.tensor_copy(tab["totals"][0:1, :], ps[0:1, 6, 2 * NE:2 * NE + 2]).then_inc(rows_ev, 1)
            link(v.tensor_scalar(V8[:, :], V8[:, :], 1.0, None, ALU.subtract))
            link(v.tensor_copy(it32[:, :], V8[:, :]))
            link(v.tensor_scalar(it32[:, :], it32[:, :], 7, None, ALU.arith_shift_right))
            link(v.tensor_copy(itf[:, :], it32[:, :]))
            link(v.scalar_tensor_tensor(pf8[:, :], itf[:, :], -float(P), V8[:, :], ALU.mult, ALU.add))
            link(v.tensor_scalar(V8[:, :], V8[:, :], 1.0, None, ALU.add))
            for t in range(T):
                for k in range(8):
                    c = t * 8 + k
                    link(v.scalar_tensor_tensor(e0[:, 0:NE], V[:, t, :], V8[:, c:c + 1], G[:, t, :], ALU.is_equal, ALU.mult, accum_out=g8[:, c:c + 1]))
                    if c >= 2:
                        v.wait_ge(ab_used, c - 1)
                    v.tensor_scalar(A[:, c % 2, :], iota[:, 0:P], pf8[:, c:c + 1], None, ALU.is_equal).then_inc(ab_done, 1)
                    v.tensor_scalar(B[:, c % 2, 0:NI], iota, itf[:, c:c + 1], cst[:, K_TOK + t:K_TOK + t + 1], ALU.is_equal, ALU.mult).then_inc(ab_done, 1)
                    v.tensor_scalar(B[:, c % 2, NI:2 * NI], iota, itf[:, c:c + 1], g8[:, c:c + 1], ALU.is_equal, ALU.mult).then_inc(ab_done, 1)
                v.wait_ge(sg_done, t + 1)
                if t:
                    v.wait_ge(ht_pe, t)
                v.tensor_tensor(hx[:, :], sg[:, :], ps[:, t % 2, DE:2 * DE], ALU.mult).then_inc(hx_done, 1)
                v.wait_ge(dn_pe, t + 1)
                v.tensor_tensor(hh[:, t, :], ps[:, 4:6, :].rearrange("p a n -> p (a n)"), hh[:, t, :], ALU.add).then_inc(acc_in, 1)
            v.wait_ge(ab_used, 64)
            link(v.tensor_scalar(e0[:, :], ps[:, 3, 0:NI], 0.0, None, ALU.is_equal))
            link(v.scalar_tensor_tensor(e0[:, :], e0[:, :], cst[:, K_PART:K_PART + 1], ps[:, 3, 0:NI], ALU.mult, ALU.add))
            link(v.tensor_scalar(e0[:, :], e0[:, :], float(S), None, ALU.add))
            link(v.tensor_copy(tab["token"][:, 0:NI], e0[:, :]))
            link(v.tensor_copy(tab["gate"][:, 0:NI], ps[:, 3, NI:2 * NI]))
            v.wait_ge(rows_ev, 4)

        @block.tensor
        def _(pe):
            mm = nc.tensor.matmul

            def transposes(t):
                pe.wait_ge(xm_done, t + 1)
                for b in range(2):
                    if t:
                        pe.wait_ge(xt_ev, 2 * (t - 1) + b + 1)
                    for k in range(4 * b, 4 * b + 4):
                        i = nc.tensor.transpose(ps[:, 4 + b, (k % 4) * P:(k % 4 + 1) * P], xm[:, t % 2, k * P:(k + 1) * P], ident)
                    i.then_inc(xt_pe, 1)

            def router(t):
                pe.wait_ge(xt_ev, 2 * (t + 1))
                if t >= 2:
                    pe.wait_ge(ex_done, t - 1)
                for k in range(KD):
                    i = mm(ps[:, 6 + t % 2, 0:NE], xmT[:, k, tok(t)], rw[:, k, :], start=k == 0, stop=k == KD - 1)
                i.then_inc(lg_pe, 1)

            pe.wait_ge(ld_w, 32)
            for t in range(T):
                if t >= 2:
                    pe.wait_ge(h_done, t - 1)
                for nh in range(2):
                    for k in range(KD):
                        i = mm(ps[:, 2 * (t % 2) + nh, :], mixT[:, k, tok(t)], wo[:, k, nh * 512:nh * 512 + 512], start=k == 0, stop=k == KD - 1)
                i.then_inc(h_pe, 1)
                if t >= 1:
                    if t == 1:
                        pe.wait_ge(ld_s, 48)
                    transposes(t - 1)
                if t >= 2:
                    router(t - 2)
            transposes(T - 1)
            router(T - 2)
            router(T - 1)
            pe.wait_ge(ex_done, T)
            for t in range(T):
                pe.wait_ge(m_done, t + 1)
                i = mm(ps[:, 7, 0:1], M[:, t, :], ones[:, 0:1], start=t == 0, stop=t == T - 1)
            i.then_inc(cnt_pe, 1)

            def shared_up(t):
                if t == 0:
                    pe.wait_ge(ld_sh, 48)
                    pe.wait_ge(h_done, T)
                if t >= 2:
                    pe.wait_ge(hx_done, t - 1)
                for k in range(KD):
                    i = mm(ps[:, t % 2, :], xmT[:, k, tok(t)], sgu[:, k, :], start=k == 0, stop=k == KD - 1)
                i.then_inc(gu_pe, 1)

            pe.wait_ge(nba_done, 1)
            i = mm(ps[:, 7, 4:6], strict, nba[:, :], start=True, stop=True)
            i.then_inc(bo_pe, 1)
            shared_up(0)
            pe.wait_ge(cols_done, 1)
            for t in range(T):
                dst = ps[:, 4 + t // 4, (t % 4) * NE:(t % 4 + 1) * NE]
                mm(dst, strict, M[:, t, :], start=True, stop=False)
                for t2 in range(t):
                    mm(dst, ones, M[:, t2, :], start=False, stop=False)
                i = mm(dst, ones, R[:, :], start=False, stop=True)
            i.then_inc(v_pe, 1)
            pe.wait_ge(cols_done, 2)
            mm(ps[0:1, 7, 8:8 + NI], ec[:, 3:4], ind[:, :], start=True, stop=True)
            mm(ps[0:1, 7, 8 + NI:8 + 2 * NI], ec[:, 4:5], ind[:, :], start=True, stop=True)
            mm(ps[0:1, 6, 0:NE], cst[:, K_PART:K_PART + 1], ind2[:, :], start=True, stop=True)
            mm(ps[0:1, 6, NE:2 * NE], ec[:, 5:6], ind2[:, :], start=True, stop=True)
            mm(ps[0:1, 6, 2 * NE:2 * NE + 1], nba[:, 0:1], ones[:, 0:1], start=True, stop=True)
            i = mm(ps[0:1, 6, 2 * NE + 1:2 * NE + 2], nba[:, 1:2], ones[:, 0:1], start=True, stop=True)
            i.then_inc(rows_pe, 1)
            for t in range(T):
                for k in range(8):
                    c = t * 8 + k
                    pe.wait_ge(ab_done, 3 * (c + 1))
                    mm(ps[:, 3, 0:2 * NI], A[:, c % 2, :], B[:, c % 2, :], start=c == 0, stop=c == 63).then_inc(ab_used, 1)
                pe.wait_ge(hx_done, t + 1)
                if t + 1 < T:
                    shared_up(t + 1)
                if t:
                    pe.wait_ge(ht_ev, t)
                for j in range(2):
                    i = nc.tensor.transpose(ps[:, 2, j * P:(j + 1) * P], hx[:, j * P:(j + 1) * P], ident)
                i.then_inc(ht_pe, 1)
                pe.wait_ge(ht_ev, t + 1)
                pe.wait_ge(acc_in, t) if t else pe.wait_ge(v_done, 1)
                for nh in range(2):
                    for j in range(2):
                        i = mm(ps[:, 4 + nh, :], hT[:, j, :], sd[:, j, nh * 512:nh * 512 + 512], start=j == 0, stop=j == 1)
                i.then_inc(dn_pe, 1)


def experts(nc, ctx, io, cst, tab, fin):
    def sb(name, shape, dt=F32):
        return ctx.enter_context(nc.sbuf_tensor(name, shape, dt))

    def sem(name):
        return ctx.enter_context(nc.semaphore(name))

    ident = cst[:, K_ID:K_ID + P]
    WG, WU, WD, WL = 0, KD * DE, 2 * KD * DE, 3 * KD * DE
    W = sb("W", [P, NW * WL])
    xg = sb("xg", [P, 2, D])
    xT = sb("xT", [P, 2, KD, P])
    sg = sb("sg3", [P, 2, P])
    hx = sb("hx3", [P, 2, P])
    hT = sb("hT3", [P, 2, P])
    y = sb("y", [P, 2, D])
    ig = sb("ig", [P, 2], I32)
    isc = sb("isc", [P, 2], I32)
    ps = ctx.enter_context(nc.psum_tensor("ps_exp", [P, 8, 512], F32))
    GU, HB, XB, YB = 0, 2, 4, 6

    w_in = [sem(f"w_in{s}") for s in range(NW)]
    xg_in = [sem(f"xg_in{s}") for s in range(2)]
    xg_used = sem("xg_used")
    xT_act, xT_dve = sem("xT_act"), sem("xT_dve")
    gu_done, sg_done, hx_done, hT_pe, hT_done = (sem(n) for n in ("gu_done", "sg_done3", "hx_done3", "hT_pe", "hT_done"))
    y_pe, y_act, y_dve = sem("y_pe"), sem("y_act"), sem("y_dve")
    added = sem("added")
    idx_c, idx_seen, x_zero = sem("idx_c"), sem("idx_seen"), sem("x_zero")
    IT = tab["item"]

    with nc.Block() as block:
        @block.sync
        def _(sp):
            n_act = sp.value_load(tab["totals"][0:1, 1:2], min_val=0, max_val=NE)
            wsrc = [io[k].rearrange("a e (p c) n -> p (a e) (c n)", c=KD) for k in ("exp_w_gate", "exp_w_up")]
            wdn = io["exp_w_down"].rearrange("a e (j p) n -> p (a e) j n", p=P)
            with sp.Fori(0, 43) as r:
                for s in range(NW):
                    n = r * NW + s
                    with sp.If(n < n_act):
                        e = sp.value_load(tab["expert"][0:1, bass.ds(n, 1)], min_val=0, max_val=NE - 1)
                        free = sp.value_load(tab["free"][0:1, bass.ds(n, 1)], min_val=1, max_val=NI)
                        sp.wait_ge(y_pe, free)
                        for src, o in ((wsrc[0], WG), (wsrc[1], WU)):
                            sp.dma_start(W[:, s * WL + o:s * WL + o + KD * DE], src[:, bass.ds(e, 1), :].rearrange("p a n -> p (a n)")).then_inc(w_in[s], 16)
                        sp.dma_start(W[:, s * WL + WD:(s + 1) * WL].rearrange("p (j n) -> p j n", j=2),
                                     wdn[:, bass.ds(e, 1), :, :].rearrange("p a j n -> p (a j) n")).then_inc(w_in[s], 16)

        @block.gpsimd
        def _(pool):
            n_items = pool.value_load(tab["totals"][0:1, 0:1], min_val=1, max_val=NI - 1)
            pool.memset(xg[:, :, :], 0.0).then_inc(x_zero, 1)
            pool.wait_ge(x_zero, 1)
            for o in (S, S + DUMP // 2):
                pool.dma_start(io["acc"][o:o + DUMP // 2, :], xg[0:DUMP // 2, 0, :]).then_inc(added, 16)
            pool.wait_ge(added, 32)

            def gather(i, s, waited):
                pool.tensor_copy(ig[:, s:s + 1], tab["token"][:, bass.ds(i, 1)]).then_inc(idx_c, 1)
                pool.wait_ge(idx_c, waited)
                pool.sem_inc(idx_seen, 1)
                pool.indirect_dma_start(out=xg[:, s, :], out_offset=None, in_=io["xm"],
                                        in_offset=bass.IndirectOffsetOnAxis(ap=ig[:, s:s + 1], axis=0),
                                        bounds_check=S - 1, oob_is_err=False).then_inc(xg_in[s], 16)

            gather(0, 0, 1)
            with pool.If(n_items > 1):
                gather(1, 1, 2)
            with pool.Else():
                pool.sem_inc(idx_c, 1)
            with pool.Fori(0, NI // 2) as r:
                for s in range(2):
                    i = r * 2 + s
                    with pool.If(i + 2 < n_items):
                        pool.wait_ge(xg_used, i + 2)
                        gather(i + 2, s, 2 * i + 3)
                    with pool.Else():
                        pool.sem_inc(idx_c, 1)
                    with pool.If(i < n_items):
                        pool.wait_ge(y_act, i + 2)
                        pool.wait_ge(y_dve, i + 2)
                        pool.wait_ge(added, 16 * i + 32)
                        pool.tensor_copy(isc[:, s:s + 1], tab["token"][:, bass.ds(i, 1)]).then_inc(idx_c, 1)
                        pool.wait_ge(idx_c, 2 * i + 4)
                        pool.sem_inc(idx_seen, 1)
                        pool.indirect_dma_start(out=io["acc"], out_offset=bass.IndirectOffsetOnAxis(ap=isc[:, s:s + 1], axis=0),
                                                in_=y[:, s, :], in_offset=None, compute_op=ALU.add).then_inc(added, 16)
                    pool.nop()
            pool.wait_ge(added, 16 * n_items + 32)

        @block.scalar
        def _(act):
            n_items = act.value_load(tab["totals"][0:1, 0:1], min_val=1, max_val=NI - 1)

            def x_half(i, s):
                act.wait_ge(xg_used, i + 2)
                act.activation(xT[:, s, 0:4, :].rearrange("p k n -> p (k n)"), ps[:, XB, :], ACT.Copy).then_inc(xT_act, 1)

            act.dma_start(fin["wg"][:, :, :], io["ple_w_gate"].rearrange("a (k p) n -> p (a k) n", p=P)).then_inc(fin["in"], 16)
            act.dma_start(fin["wi"][:, :, :], io["ple_w_in"].rearrange("a (j p) n -> p (a j) n", p=P)).then_inc(fin["in"], 16)
            act.dma_start(fin["gains"][:, 0, :], io["ple_norm_g"].to_broadcast([P, D])).then_inc(fin["in"], 16)
            act.dma_start(fin["gains"][:, 1, :], io["final_norm_g"].rearrange("(a n) -> a n", a=1).to_broadcast([P, D])).then_inc(fin["in"], 16)
            act.sem_inc(y_act, 1)
            x_half(0, 0)
            with act.Fori(0, NI // 2) as r:
                for s in range(2):
                    i = r * 2 + s
                    with act.If(i < n_items):
                        for j in range(2):
                            act.wait_ge(gu_done, 2 * i + j + 1)
                            act.activation(sg[:, j, :], ps[:, GU + j, 0:P], ACT.Silu).then_inc(sg_done, 1)
                        with act.If(i + 1 < n_items):
                            x_half(i + 1, 1 - s)
                        act.wait_ge(y_pe, i + 2)
                        act.wait_ge(added, 16 * i + 16)
                        act.activation(y[:, s, 0:512], ps[:, YB, :], ACT.Copy, scale=tab["gate"][:, bass.ds(i, 1)]).then_inc(y_act, 1)
                    act.nop()

        @block.vector
        def _(v):
            n_items = v.value_load(tab["totals"][0:1, 0:1], min_val=1, max_val=NI - 1)

            def x_half(i, s):
                v.wait_ge(xg_used, i + 2)
                v.tensor_copy(xT[:, s, 4:8, :].rearrange("p k n -> p (k n)"), ps[:, XB + 1, :]).then_inc(xT_dve, 1)

            v.sem_inc(y_dve, 1)
            x_half(0, 0)
            with v.Fori(0, NI // 2) as r:
                for s in range(2):
                    i = r * 2 + s
                    with v.If(i < n_items):
                        for j in range(2):
                            v.wait_ge(sg_done, 2 * i + j + 1)
                            v.tensor_tensor(hx[:, j, :], sg[:, j, :], ps[:, GU + j, P:2 * P], ALU.mult).then_inc(hx_done, 1)
                        with v.If(i + 1 < n_items):
                            x_half(i + 1, 1 - s)
                        for j in range(2):
                            v.wait_ge(hT_pe, 2 * i + j + 1)
                            v.tensor_copy(hT[:, j, :], ps[:, HB + j, 0:P]).then_inc(hT_done, 1)
                        v.wait_ge(y_pe, i + 2)
                        v.wait_ge(added, 16 * i + 16)
                        v.tensor_scalar(y[:, s, 512:D], ps[:, YB + 1, :], tab["gate"][:, bass.ds(i, 1)], None, ALU.mult).then_inc(y_dve, 1)
                    v.nop()

        @block.tensor
        def _(pe):
            mm = nc.tensor.matmul
            pe.sem_inc(y_pe, 1)
            pe.sem_inc(xg_used, 1)
            n_items = pe.value_load(tab["totals"][0:1, 0:1], min_val=1, max_val=NI - 1)

            def x_transposes(s):
                for k in range(KD):
                    last = nc.tensor.transpose(ps[:, XB + k // 4, (k % 4) * P:(k % 4 + 1) * P],
                                               xg[:, s, :].rearrange("p (q k) -> p k q", k=KD)[:, k, :], ident)
                last.then_inc(xg_used, 1)

            pe.wait_ge(xg_in[0], 16)
            x_transposes(0)
            with pe.Fori(0, NI // 2) as r:
                for s in range(2):
                    i = r * 2 + s
                    with pe.If(i < n_items):
                        slot = pe.value_load(IT[0:1, bass.ds(i, 1), 0:1], min_val=0, max_val=NW - 1)
                        landed = pe.value_load(IT[0:1, bass.ds(i, 1), 1:2], min_val=48, max_val=48 * 43)
                        with pe.If(slot < 1):
                            pe.wait_ge(w_in[0], landed)
                        with pe.Else():
                            with pe.If(slot < 2):
                                pe.wait_ge(w_in[1], landed)
                            with pe.Else():
                                pe.wait_ge(w_in[2], landed)
                            pe.nop()
                        base = pe.snap(slot * WL)
                        pe.wait_ge(xT_act, i + 1)
                        pe.wait_ge(xT_dve, i + 1)
                        for j in range(2):
                            for k in range(KD):
                                rhs = two_columns(W, base + (k * DE + j * P), KD * DE)
                                last = mm(ps[:, GU + j, 0:2 * P].rearrange("p (a n) -> p a n", a=2), xT[:, s, k, :], rhs, start=k == 0, stop=k == KD - 1)
                            last.then_inc(gu_done, 1)
                        with pe.If(i + 1 < n_items):
                            pe.wait_ge(xg_in[1 - s], 16 * (r + 1) + 16 * s)
                            x_transposes(1 - s)
                        for j in range(2):
                            pe.wait_ge(hx_done, 2 * i + j + 1)
                            nc.tensor.transpose(ps[:, HB + j, 0:P], hx[:, j, :], ident).then_inc(hT_pe, 1)
                        pe.wait_ge(hT_done, 2 * i + 2)
                        pe.wait_ge(y_act, i + 1)
                        pe.wait_ge(y_dve, i + 1)
                        for nh in range(2):
                            for j in range(2):
                                last = mm(ps[:, YB + nh, :], hT[:, j, :], W[:, bass.ds(base + (WD + j * D + nh * 512), 512)], start=j == 0, stop=j == 1)
                        last.then_inc(y_pe, 1)
                    pe.nop()


def two_columns(W, at, step):
    return W[:, bass.ds(at, 2 * step)].rearrange("p (a n) -> p a n", a=2)[:, :, 0:P]


def finish(nc, ctx, io, cst, fin, out):
    def sb(name, shape, dt=F32):
        return ctx.enter_context(nc.sbuf_tensor(name, shape, dt))

    def sem(name):
        return ctx.enter_context(nc.semaphore(name))

    ident = cst[:, K_ID:K_ID + P]
    h2 = sb("h2", [P, 2, D])
    pt = sb("pt", [P, 2, PLE])
    hT, pT = sb("h2T", [P, 2, KD, P]), sb("pT", [P, 2, 2, P])
    gate = sb("gate4", [P, 2, D])
    r, scratch, o = sb("r4", [P, D]), sb("scratch4", [P, D]), sb("o4", [P, 2, D])
    sq = sb("sq4", [P, 2 * T])
    ps = ctx.enter_context(nc.psum_tensor("ps_fin", [P, 8, 512], F32))
    h_in = [sem(f"f_in{i}") for i in range(2)]
    t_pe, t_act, t_dve, g_pe, sg_done, r_done, sq_done, sd_done, chain, h3_done, o_done = (
        sem("f_" + n) for n in ("t_pe", "t_act", "t_dve", "g_pe", "sg", "r", "sq", "sd", "chain", "h3", "o"))
    stored = [sem(f"f_st{i}") for i in range(2)]

    def tok(t):
        return slice(t * P, (t + 1) * P)

    with nc.Block() as block:
        @block.sync
        def _(sp):
            for t in range(T):
                if t >= 2:
                    sp.wait_ge(h3_done, t - 1)
                sp.dma_start(h2[:, t % 2, :], io["acc"][tok(t), :]).then_inc(h_in[t % 2], 16)
                sp.dma_start(pt[:, t % 2, :], io["p"][0, 0, tok(t), :]).then_inc(h_in[t % 2], 16)
                if t >= 1:
                    sp.wait_ge(o_done, t)
                    sp.dma_start(out[0, tok(t - 1), :], o[:, (t - 1) % 2, :]).then_inc(stored[(t - 1) % 2], 16)
            sp.wait_ge(o_done, T)
            sp.dma_start(out[0, tok(T - 1), :], o[:, (T - 1) % 2, :]).then_inc(stored[(T - 1) % 2], 16)
            for b in range(2):
                sp.wait_ge(stored[b], 16 * (T // 2))

        @block.scalar
        def _(act):
            act.wait_ge(fin["in"], 64)
            for t in range(T):
                act.wait_ge(t_pe, t + 1)
                if t >= 2:
                    act.wait_ge(g_pe, t - 1)
                act.activation(hT[:, t % 2, 0:4, :].rearrange("p k n -> p (k n)"), ps[:, 0, :], ACT.Copy).then_inc(t_act, 1)
                act.activation(pT[:, t % 2, :, :].rearrange("p k n -> p (k n)"), ps[:, 2, 0:PLE], ACT.Copy).then_inc(t_act, 1)
                act.wait_ge(g_pe, t + 1)
                for nh in range(2):
                    act.activation(gate[:, t % 2, nh * 512:nh * 512 + 512], ps[:, 4 + nh, :], ACT.Sigmoid).then_inc(sg_done, 1)
                for j in range(2):
                    act.wait_ge(r_done, 2 * t + j + 1)
                    act.activation(scratch[:, :], r[:, :], ACT.Square, accum_out=sq[:, 2 * t + j:2 * t + j + 1]).then_inc(sq_done, 1)
                    act.wait_ge(sq_done, 2 * t + j + 1)
                    act.activation(sq[:, 2 * t + j:2 * t + j + 1], sq[:, 2 * t + j:2 * t + j + 1], ACT.Sqrt,
                                   bias=cst[:, K_EPS:K_EPS + 1], scale=1.0 / D).then_inc(sd_done, 1)

        @block.vector
        def _(v):
            n = [0]

            def link(i):
                n[0] += 1
                i.then_inc(chain, 1)
                v.wait_ge(chain, n[0])

            v.wait_ge(fin["in"], 64)
            for t in range(T):
                v.wait_ge(t_pe, t + 1)
                if t >= 2:
                    v.wait_ge(g_pe, t - 1)
                v.tensor_copy(hT[:, t % 2, 4:8, :].rearrange("p k n -> p (k n)"), ps[:, 1, :]).then_inc(t_dve, 1)
                v.wait_ge(sg_done, 2 * t + 2)
                v.tensor_tensor(r[:, :], ps[:, 6:8, :].rearrange("p a n -> p (a n)"), gate[:, t % 2, :], ALU.mult).then_inc(r_done, 1)
                v.wait_ge(sd_done, 2 * t + 1)
                a = sq[:, 2 * t:2 * t + 1]
                link(v.reciprocal(a, a))
                link(v.scalar_tensor_tensor(r[:, :], r[:, :], a, fin["gains"][:, 0, :], ALU.mult, ALU.mult))
                link(v.tensor_tensor(r[:, :], r[:, :], h2[:, t % 2, :], ALU.add))
                v.sem_inc(h3_done, 1)
                v.sem_inc(r_done, 1)
                v.wait_ge(sd_done, 2 * t + 2)
                a = sq[:, 2 * t + 1:2 * t + 2]
                link(v.reciprocal(a, a))
                if t >= 2:
                    v.wait_ge(stored[t % 2], 16 * (t // 2))
                link(v.scalar_tensor_tensor(o[:, t % 2, :], r[:, :], a, fin["gains"][:, 1, :], ALU.mult, ALU.mult))
                v.sem_inc(o_done, 1)

        @block.tensor
        def _(pe):
            mm = nc.tensor.matmul

            def transposes(t):
                pe.wait_ge(h_in[t % 2], 32 * (t // 2 + 1))
                if t:
                    pe.wait_ge(t_act, 2 * t)
                    pe.wait_ge(t_dve, t)
                for k in range(KD):
                    nc.tensor.transpose(ps[:, k // 4, (k % 4) * P:(k % 4 + 1) * P], h2[:, t % 2, k * P:(k + 1) * P], ident)
                for j in range(2):
                    i = nc.tensor.transpose(ps[:, 2, j * P:(j + 1) * P], pt[:, t % 2, j * P:(j + 1) * P], ident)
                i.then_inc(t_pe, 1)

            pe.wait_ge(fin["in"], 64)
            transposes(0)
            for t in range(T):
                if t + 1 < T:
                    transposes(t + 1)
                pe.wait_ge(t_act, 2 * t + 2)
                pe.wait_ge(t_dve, t + 1)
                if t:
                    pe.wait_ge(r_done, 2 * t - 1)
                for nh in range(2):
                    for k in range(KD):
                        mm(ps[:, 4 + nh, :], hT[:, t % 2, k, :], fin["wg"][:, k, nh * 512:nh * 512 + 512], start=k == 0, stop=k == KD - 1)
                for nh in range(2):
                    for j in range(2):
                        i = mm(ps[:, 6 + nh, :], pT[:, t % 2, j, :], fin["wi"][:, j, nh * 512:nh * 512 + 512], start=j == 0, stop=j == 1)
                i.then_inc(g_pe, 1)


def build(nc, io, out):
    io["xm"] = nc.dram_tensor("xm_rows", (S, D), F32, kind="Internal").ap()
    io["acc"] = nc.dram_tensor("acc_rows", (S + DUMP, D), F32, kind="Internal").ap()
    with ExitStack() as ctx:
        def sb(name, shape, dt=F32):
            return ctx.enter_context(nc.sbuf_tensor(name, shape, dt))

        cst = sb("cst", [P, K_LEN])
        tab = {"token": sb("tab_token", [P, NI + 8], I32), "gate": sb("tab_gate", [P, NI + 8]),
               "item": sb("tab_item", [1, NI + 8, 2], I32), "expert": sb("tab_expert", [1, NE + 8], I32),
               "free": sb("tab_free", [1, NE + 8], I32), "totals": sb("tab_totals", [1, 2], I32)}
        with ExitStack() as c:
            mixT = c.enter_context(nc.sbuf_tensor("mixT", [P, KD, S], F32))
            with ExitStack() as c2:
                mixers(nc, c2, io, cst, mixT)
            with ExitStack() as c2:
                route(nc, c2, io, cst, mixT, tab)
        fin = {"wg": sb("ple_gate", [P, KD, D]), "wi": sb("ple_in", [P, 2, D]), "gains": sb("gains", [P, 2, D]),
               "in": ctx.enter_context(nc.semaphore("fin_in"))}
        with ExitStack() as c:
            experts(nc, c, io, cst, tab, fin)
        with ExitStack() as c:
            finish(nc, c, io, cst, fin, out)


INPUTS = ("x", "p", "norm1_g", "w_in", "four_w", "gmlp_ln_g", "gmlp_ln_b", "gmlp_ws", "gmlp_bs", "mlstm_conv_w",
          "mlstm_gate_b", "mlstm_norm_g", "w_out", "norm2_g", "router_w", "router_b", "exp_w_gate", "exp_w_up",
          "exp_w_down", "sh_w_gate", "sh_w_up", "sh_w_down", "ple_w_in", "ple_w_gate", "ple_norm_g", "final_norm_g")


def kernel(**inputs):
    import concourse.bacc as bacc
    from concourse.bass_utils import run_bass_kernel_spmd

    nc = bacc.Bacc("TRN2", target_bir_lowering=False, num_devices=1)
    consts, dft = shape_constants()
    arrays = {f"in_{k}": np.ascontiguousarray(inputs[k]) for k in INPUTS}
    arrays["in_consts"], arrays["in_dft"] = consts, dft
    io = {k[3:]: nc.dram_tensor(k, a.shape, mybir.dt.from_np(a.dtype), kind="ExternalInput").ap() for k, a in arrays.items()}
    out = nc.dram_tensor("out", (1, S, D), F32, kind="ExternalOutput").ap()
    build(nc, io, out)
    r = run_bass_kernel_spmd(nc, [arrays], core_ids=[0])
    return r.results[0]["out"]
```
